# Optimizing a Trainium2 kernel written in Bass

```python
import jax, jax.numpy as jnp
from jax import lax
import numpy as np

D_MODEL = 1024
BATCH = 1
SEQ = 1024
DEPTH = 1
DEC_BATCH = 8
DEC_SEQ = 1
PAST_LEN = 4096
PAGE_SIZE = 128

N_META = 16
SB_HEADS = 8
SB_HEAD_DIM = 64
SB_WIDTH = SB_HEADS * SB_HEAD_DIM
SB_BLOCK = 128
SB_SCALE = SB_HEAD_DIM ** -0.5
SB_BIAS_INIT = -6.0
HG_HEADS = 4
HG_DK = 128
HG_DV = 128
HG_KW = HG_HEADS * HG_DK
HG_VW = HG_HEADS * HG_DV
HG_CHUNK = 64
HG_SCALE = HG_DK ** -0.5
MIX_WIDTH = SB_WIDTH + HG_VW
IN_WIDTH = 3 * SB_WIDTH + 2 * HG_KW + 2 * HG_VW
SPLITS = (SB_WIDTH, 2 * SB_WIDTH, 3 * SB_WIDTH, 3 * SB_WIDTH + HG_KW,
          3 * SB_WIDTH + 2 * HG_KW, 3 * SB_WIDTH + 2 * HG_KW + HG_VW)
PEER_HEADS = 8
PEER_N_KEYS = 128
PEER_N_EXPERTS = PEER_N_KEYS * PEER_N_KEYS
PEER_QDIM = 256
PEER_HALF = PEER_QDIM // 2
PEER_TOPK = 16
PEER_BLOCK = 128
DN_ALPHA = (2.0 * DEPTH) ** 0.25
DN_BETA = (8.0 * DEPTH) ** -0.25
EPS = 1e-5

kernel_name = 'hymba_sb_hgrn2_peer_step'

F32 = jnp.float32

def layer_norm(x, g, b):
    xf = x.astype(F32)
    mu = jnp.mean(xf, -1, keepdims=True)
    xc = xf - mu
    var = jnp.mean(xc * xc, -1, keepdims=True)
    return xc * lax.rsqrt(var + EPS) * g.astype(F32) + b.astype(F32)

def rms_norm(x, g):
    xf = x.astype(F32)
    return xf * lax.rsqrt(jnp.mean(xf * xf, -1, keepdims=True) + EPS) * g.astype(F32)

def post_ln(x, delta, g, b, dtype):
    return layer_norm(DN_ALPHA * x.astype(F32) + delta.astype(F32), g, b).astype(dtype)

def in_proj(xn, w):
    p = jnp.einsum('bld,de->ble', xn, w)
    b, l, _ = p.shape
    q_sb, k_sb, v_sb, q_hg, f_hg, i_hg, g_hg = jnp.split(p, SPLITS, axis=-1)
    sbh = lambda a: a.reshape(b, l, SB_HEADS, SB_HEAD_DIM)
    hgh = lambda a, d: jnp.swapaxes(a.reshape(b, l, HG_HEADS, d), 1, 2).astype(F32)
    return (sbh(q_sb), sbh(k_sb), sbh(v_sb), hgh(q_hg, HG_DK), hgh(f_hg, HG_DK),
            hgh(i_hg, HG_DV), g_hg)

def hgrn_gates(q_raw, f_raw, lb):
    lb = lb.reshape(HG_HEADS, 1, HG_DK)
    log_f = jnp.logaddexp(jnp.log(lb), jnp.log1p(-lb) + jax.nn.log_sigmoid(f_raw))
    k = (1.0 - lb) * jax.nn.sigmoid(-f_raw)
    q = jax.nn.silu(q_raw) * HG_SCALE
    return q, k, log_f

def hgrn_chunk(S, q, k, log_f, v):
    c = q.shape[2]
    G = jnp.cumsum(log_f, axis=2)
    causal = jnp.tril(jnp.ones((c, c), bool))[:, :, None]
    diff = G[:, :, :, None, :] - G[:, :, None, :, :]
    decay = jnp.exp(jnp.where(causal, diff, -jnp.inf))
    scores = jnp.einsum('bhtk,bhsk,bhtsk->bhts', q, k, decay)
    o = (jnp.einsum('bhts,bhsv->bhtv', scores, v)
         + jnp.einsum('bhtk,bhkv->bhtv', q * jnp.exp(G), S))
    G_last = G[:, :, -1:, :]
    S_new = (jnp.exp(G_last[:, :, 0, :, None]) * S
             + jnp.einsum('bhsk,bhsv->bhkv', k * jnp.exp(G_last - G), v))
    return o, S_new

def hgrn_prompt(q, k, log_f, v):
    b = q.shape[0]
    S0 = jnp.zeros((b, HG_HEADS, HG_DK, HG_DV), F32)
    o_meta, S = hgrn_chunk(S0, q[:, :, :N_META], k[:, :, :N_META], log_f[:, :, :N_META], v[:, :, :N_META])

    def to_chunks(a):
        a = a[:, :, N_META:]
        bb, hh, ll, dd = a.shape
        return jnp.moveaxis(a.reshape(bb, hh, ll // HG_CHUNK, HG_CHUNK, dd), 2, 0)

    def body(S, xs):
        qc, kc, fc, vc = xs
        o, S = hgrn_chunk(S, qc, kc, fc, vc)
        return S, o

    S, o_real = lax.scan(body, S, (to_chunks(q), to_chunks(k), to_chunks(log_f), to_chunks(v)))
    o_real = jnp.moveaxis(o_real, 0, 2).reshape(b, HG_HEADS, SEQ, HG_DV)
    return jnp.concatenate([o_meta, o_real], axis=2), S

def sb_attend(q, k, v, bias, pos_q, pos_k):
    z = (jnp.einsum('bqhd,bkhd->bhqk', q.astype(F32), k.astype(F32)) * SB_SCALE
         + bias.astype(F32)[None, :, None, None])
    mask = pos_k[None, :] < pos_q[:, None]
    sp = jnp.where(mask, jax.nn.softplus(z), 0.0)
    after = lax.cumsum(sp, axis=3, reverse=True) - sp
    w = jnp.where(mask, jnp.exp(jax.nn.log_sigmoid(z) - after), 0.0)
    return jnp.einsum('bhqk,bkhd->bqhd', w, v.astype(F32))

def sb_prompt(q, k, v, bias):
    b = q.shape[0]
    pos = jnp.arange(N_META + SEQ)
    o_meta = sb_attend(q[:, :N_META], k[:, :N_META], v[:, :N_META], bias, pos[:N_META], pos[:N_META])
    nb = SEQ // SB_BLOCK
    q_blocks = jnp.moveaxis(q[:, N_META:].reshape(b, nb, SB_BLOCK, SB_HEADS, SB_HEAD_DIM), 1, 0)

    def blk(args):
        qb, bi = args
        pos_q = N_META + bi * SB_BLOCK + jnp.arange(SB_BLOCK)
        return sb_attend(qb, k, v, bias, pos_q, pos)

    o_real = lax.map(blk, (q_blocks, jnp.arange(nb)))
    o_real = jnp.moveaxis(o_real, 0, 1).reshape(b, SEQ, SB_HEADS, SB_HEAD_DIM)
    return jnp.concatenate([o_meta, o_real], axis=1)

def mix_out(o_sb, o_hg, g_hg, sb_g, hg_g, w_out):
    b, l = o_sb.shape[:2]
    sb = rms_norm(o_sb.reshape(b, l, SB_WIDTH), sb_g)
    hg = rms_norm(jnp.swapaxes(o_hg, 1, 2), hg_g.reshape(HG_HEADS, HG_DV)).reshape(b, l, HG_VW)
    hg = hg * jax.nn.silu(g_hg.astype(F32))
    return jnp.einsum('ble,ed->bld', jnp.concatenate([sb, hg], axis=-1), w_out.astype(F32))

def peer_block(h, w_pq, sub_keys, expert_u, expert_v):
    n = h.shape[0]
    q = jnp.einsum('nd,de->ne', h.astype(F32), w_pq.astype(F32)).reshape(n, PEER_HEADS, 2, PEER_HALF)
    q = q - jnp.mean(q, -1, keepdims=True)
    q = q * lax.rsqrt(jnp.mean(q * q, -1, keepdims=True) + EPS)
    s = jnp.einsum('nhpc,hpkc->nhpk', q, sub_keys.astype(F32))
    s_top, i_top = lax.top_k(s, PEER_TOPK)
    cand = s_top[:, :, 0, :, None] + s_top[:, :, 1, None, :]
    sc, ci = lax.top_k(cand.reshape(n, PEER_HEADS, PEER_TOPK * PEER_TOPK), PEER_TOPK)
    i1 = jnp.take_along_axis(i_top[:, :, 0], ci // PEER_TOPK, axis=-1)
    i2 = jnp.take_along_axis(i_top[:, :, 1], ci % PEER_TOPK, axis=-1)
    e = i1 * PEER_N_KEYS + i2
    gate = jax.nn.softmax(sc, axis=-1)
    act = jax.nn.gelu(jnp.einsum('nd,nhkd->nhk', h.astype(F32), expert_u[e].astype(F32)), approximate=False)
    return jnp.einsum('nhk,nhkd->nd', gate * act, expert_v[e].astype(F32))

def peer(h, w_pq, sub_keys, expert_u, expert_v):
    shape = h.shape
    h2 = h.reshape(-1, D_MODEL)
    n = h2.shape[0]
    nb = -(-n // PEER_BLOCK)
    hp = jnp.pad(h2, ((0, nb * PEER_BLOCK - n), (0, 0)))
    out = lax.map(lambda hb: peer_block(hb, w_pq, sub_keys, expert_u, expert_v),
                  hp.reshape(nb, PEER_BLOCK, D_MODEL))
    return out.reshape(nb * PEER_BLOCK, D_MODEL)[:n].reshape(shape)

def setup_inputs(seed: int = 0) -> dict:
    key = jax.random.key(seed)
    ks = jax.random.split(key, 24)
    n_pages = PAST_LEN // PAGE_SIZE
    n_used = DEC_BATCH * n_pages
    n_phys = (5 * n_used) // 4

    def nrm(k, shape, scale):
        return jax.random.normal(k, shape, F32) * scale

    x_prompt = nrm(ks[0], (BATCH, SEQ, D_MODEL), 1.0)
    x_sample = nrm(ks[1], (DEC_BATCH, DEC_SEQ, D_MODEL), 1.0)
    cache_k = nrm(ks[2], (DEPTH, n_phys, PAGE_SIZE, SB_HEADS, SB_HEAD_DIM), 1.0)
    cache_v = nrm(ks[3], (DEPTH, n_phys, PAGE_SIZE, SB_HEADS, SB_HEAD_DIM), 1.0)
    state_hgrn = nrm(ks[4], (DEPTH, DEC_BATCH, HG_HEADS, HG_DK, HG_DV), 0.5)
    page_table = jax.random.permutation(ks[5], n_phys)[:n_used].reshape(DEC_BATCH, n_pages).astype(jnp.int32)
    meta_tokens = nrm(ks[6], (N_META, D_MODEL), 1.0)
    emb_ln_g = 1.0 + nrm(ks[7], (D_MODEL,), 0.02)
    emb_ln_b = nrm(ks[8], (D_MODEL,), 0.02)
    w_in = nrm(ks[9], (DEPTH, D_MODEL, IN_WIDTH), D_MODEL ** -0.5)
    w_in = w_in.at[:, :, 2 * SB_WIDTH:3 * SB_WIDTH].multiply(DN_BETA)
    sb_bias = SB_BIAS_INIT + nrm(ks[22], (DEPTH, SB_HEADS), 0.1)
    lb_param = nrm(ks[10], (DEPTH + 1, HG_KW), 0.1)
    sb_norm_g = 1.0 + nrm(ks[11], (DEPTH, SB_WIDTH), 0.02)
    hg_norm_g = 1.0 + nrm(ks[12], (DEPTH, HG_VW), 0.02)
    w_out = nrm(ks[13], (DEPTH, MIX_WIDTH, D_MODEL), MIX_WIDTH ** -0.5 * DN_BETA)
    ln1_g = 1.0 + nrm(ks[14], (DEPTH, D_MODEL), 0.02)
    ln1_b = nrm(ks[15], (DEPTH, D_MODEL), 0.02)
    w_pq = nrm(ks[16], (DEPTH, D_MODEL, PEER_HEADS * PEER_QDIM), D_MODEL ** -0.5)
    peer_sub_keys = nrm(ks[17], (DEPTH, PEER_HEADS, 2, PEER_N_KEYS, PEER_HALF), PEER_HALF ** -0.5)
    peer_u = nrm(ks[18], (DEPTH, PEER_N_EXPERTS, D_MODEL), D_MODEL ** -0.5)
    peer_v = nrm(ks[19], (DEPTH, PEER_N_EXPERTS, D_MODEL), DN_BETA)
    ln2_g = 1.0 + nrm(ks[20], (DEPTH, D_MODEL), 0.02)
    ln2_b = nrm(ks[21], (DEPTH, D_MODEL), 0.02)
    return {'x_prompt': x_prompt, 'x_sample': x_sample, 'cache_k': cache_k, 'cache_v': cache_v,
            'state_hgrn': state_hgrn, 'page_table': page_table, 'meta_tokens': meta_tokens,
            'emb_ln_g': emb_ln_g, 'emb_ln_b': emb_ln_b, 'w_in': w_in, 'sb_bias': sb_bias,
            'lb_param': lb_param, 'sb_norm_g': sb_norm_g, 'hg_norm_g': hg_norm_g, 'w_out': w_out,
            'ln1_g': ln1_g, 'ln1_b': ln1_b, 'w_pq': w_pq, 'peer_sub_keys': peer_sub_keys,
            'peer_u': peer_u, 'peer_v': peer_v, 'ln2_g': ln2_g, 'ln2_b': ln2_b}

def reference(x_prompt, x_sample, cache_k, cache_v, state_hgrn, page_table, meta_tokens,
              emb_ln_g, emb_ln_b, w_in, sb_bias, lb_param, sb_norm_g, hg_norm_g, w_out, ln1_g,
              ln1_b, w_pq, peer_sub_keys, peer_u, peer_v, ln2_g, ln2_b):
    dt = x_prompt.dtype
    b = x_prompt.shape[0]
    db, t = x_sample.shape[0], x_sample.shape[1]
    n_past = page_table.shape[1] * cache_k.shape[2]
    lb_all = jnp.cumsum(jax.nn.softmax(lb_param.astype(F32), axis=0), axis=0)

    meta = jnp.broadcast_to(meta_tokens.astype(dt)[None], (b, N_META, D_MODEL))
    xp = layer_norm(jnp.concatenate([meta, x_prompt], axis=1), emb_ln_g, emb_ln_b).astype(dt)
    xs = layer_norm(x_sample, emb_ln_g, emb_ln_b).astype(x_sample.dtype)

    kp_rows, vp_rows, sp_rows, ks_rows, vs_rows, ss_rows = [], [], [], [], [], []
    pos_q_s = n_past + jnp.arange(t)
    pos_k_s = jnp.arange(n_past + t)
    for l in range(DEPTH):
        q_sb, k_sb, v_sb, q_hg, f_hg, i_hg, g_hg = in_proj(xp, w_in[l])
        q_h, k_h, lf_h = hgrn_gates(q_hg, f_hg, lb_all[l])
        o_sb = sb_prompt(q_sb, k_sb, v_sb, sb_bias[l])
        o_hg, s_p = hgrn_prompt(q_h, k_h, lf_h, i_hg)
        hp = post_ln(xp, mix_out(o_sb, o_hg, g_hg, sb_norm_g[l], hg_norm_g[l], w_out[l]),
                     ln1_g[l], ln1_b[l], dt)
        if l == DEPTH - 1:
            hp = hp[:, N_META:]
        xp = post_ln(hp, peer(hp, w_pq[l], peer_sub_keys[l], peer_u[l], peer_v[l]),
                     ln2_g[l], ln2_b[l], dt)
        kp_rows.append(k_sb)
        vp_rows.append(v_sb)
        sp_rows.append(s_p.astype(state_hgrn.dtype))

        q_sb, k_sb, v_sb, q_hg, f_hg, i_hg, g_hg = in_proj(xs, w_in[l])
        q_h, k_h, lf_h = hgrn_gates(q_hg, f_hg, lb_all[l])
        past_k = cache_k[l][page_table].reshape(db, n_past, SB_HEADS, SB_HEAD_DIM)
        past_v = cache_v[l][page_table].reshape(db, n_past, SB_HEADS, SB_HEAD_DIM)
        k_all = jnp.concatenate([past_k, k_sb.astype(past_k.dtype)], axis=1)
        v_all = jnp.concatenate([past_v, v_sb.astype(past_v.dtype)], axis=1)
        o_sb = sb_attend(q_sb, k_all, v_all, sb_bias[l], pos_q_s, pos_k_s)
        o_hg, s_s = hgrn_chunk(state_hgrn[l].astype(F32), q_h, k_h, lf_h, i_hg)
        hs = post_ln(xs, mix_out(o_sb, o_hg, g_hg, sb_norm_g[l], hg_norm_g[l], w_out[l]),
                     ln1_g[l], ln1_b[l], xs.dtype)
        xs = post_ln(hs, peer(hs, w_pq[l], peer_sub_keys[l], peer_u[l], peer_v[l]),
                     ln2_g[l], ln2_b[l], xs.dtype)
        ks_rows.append(k_sb)
        vs_rows.append(v_sb)
        ss_rows.append(s_s.astype(state_hgrn.dtype))

    y_prompt = xp
    y_sample = xs
    k_prompt = jnp.stack(kp_rows, axis=0)
    v_prompt = jnp.stack(vp_rows, axis=0)
    s_prompt = jnp.stack(sp_rows, axis=0)
    k_sample = jnp.stack(ks_rows, axis=0)
    v_sample = jnp.stack(vs_rows, axis=0)
    s_sample = jnp.stack(ss_rows, axis=0)
    return (y_prompt, y_sample, k_prompt, v_prompt, s_prompt, k_sample, v_sample, s_sample)


_drawn_inputs = setup_inputs


def setup_inputs(seed=0):
    import zlib

    import numpy as np

    out = dict(_drawn_inputs(seed))
    spreads = {}
    factors = {'hg_norm_g': 3.011, 'ln2_g': 8.665, 'ln2_b': 8.089, 'sb_norm_g': 2.679}
    for name, (base, spread) in spreads.items():
        noise = np.random.default_rng([zlib.crc32(name.encode()), seed]).standard_normal(out[name].shape)
        drawn = base * np.exp(spread * noise) if base else spread * noise
        out[name] = __import__('jax').numpy.asarray(drawn.astype(out[name].dtype))
    for name, factor in factors.items():
        out[name] = (out[name] * factor).astype(out[name].dtype)
    return out
```

```python
import concourse.bass as bass
from concourse import mybir
from contextlib import ExitStack, contextmanager

F32 = mybir.dt.float32
I32 = mybir.dt.int32
U32 = mybir.dt.uint32
ALU = mybir.AluOpType
ACT = mybir.ActivationFunctionType
AX = mybir.AxisListType

P = 128
D = 1024
SEQ, N_META, N_SAMPLE = 1024, 16, 8
N_PROMPT = N_META + SEQ
SAMPLE0 = N_PROMPT
N_ROWS = SAMPLE0 + N_SAMPLE
NB = -(-N_ROWS // P)
ROWS = NB * P
MIX_ROWS = N_META + NB * P
SB_HEADS, SB_DIM = 8, 64
SB_WIDTH = SB_HEADS * SB_DIM
HG_HEADS, HG_D = 4, 128
HG_WIDTH = HG_HEADS * HG_D
Q_SB, K_SB, V_SB, Q_HG, F_HG, I_HG, G_HG = (n * 512 for n in range(7))
IN_WIDTH = 7 * 512
DC = D // P
EPS = 1e-5
SB_SCALE = SB_DIM ** -0.5
HG_SCALE = HG_D ** -0.5
DN_ALPHA = 2.0 ** 0.25
PEER_HEADS, N_KEYS, TOPK, HALF = 8, 128, 16, 128
QW = PEER_HEADS * 2 * HALF
Z_CAP = 60.0
LOWEST = -3.0e38


@contextmanager
def stage_semaphores(nc, prefix):
    mine = []

    def sem(name):
        mine.append(nc.alloc_semaphore(name=prefix + name))
        return mine[-1]

    yield sem
    nc.clear_and_free_semaphores(mine)
    nc.all_engine_barrier()


def layer_norm_stats(nc, dve, stats, mean_var, x):
    nc.vector.bn_stats(stats[:, 0:6], x[:, 0:512])
    nc.vector.bn_stats(stats[:, 6:12], x[:, 512:1024])
    dve.drain()
    nc.vector.bn_aggr(mean_var, stats[:, :])
    dve.drain()


def normalise(nc, dve, out, x, mean, rstd, gain, shift):
    nc.vector.tensor_scalar(out, x, mean, rstd, ALU.subtract, ALU.mult)
    dve.drain()
    nc.vector.tensor_tensor(out, out, gain, ALU.mult)
    dve.drain()
    return nc.vector.tensor_tensor(out, out, shift, ALU.add)


def identity_matrix(nc, pool, m):
    nc.gpsimd.memset(m, 0.0)
    pool.drain()
    nc.gpsimd.affine_select(out=m, in_=m, compare_op=ALU.not_equal, fill=1.0, base=0,
                            pattern=[[-1, m.shape[1]]], channel_multiplier=1)


def embed_and_project(nc, io, scr):
    w_in = io["w_in"][0].rearrange("(c p) n -> p c n", p=P)
    xp, xs, meta = io["x_prompt"][0], io["x_sample"].rearrange("b t d -> (b t) d"), io["meta_tokens"]
    xn_scr, proj = scr["xn"], scr["proj"]
    W = 256
    first = P - N_META
    last = N_PROMPT - (NB - 1) * P
    with ExitStack() as ctx:
        sb = lambda n, s, d=F32: ctx.enter_context(nc.sbuf_tensor("pj_" + n, s, d))
        pb = lambda n, s: ctx.enter_context(nc.psum_tensor("pj_" + n, s, F32))
        sem = ctx.enter_context(stage_semaphores(nc, "pj_"))
        x = sb("x", [P, NB, D])
        xnT = sb("xnT", [P, DC, ROWS])
        xn = [sb(f"xn{u}", [P, D]) for u in range(3)]
        w = [sb(f"w{h}", [P, DC, W]) for h in range(2)]
        stage = [sb(f"stage{h}", [P, NB, W]) for h in range(2)]
        gain, shift = sb("gain", [P, D]), sb("shift", [P, D])
        zero = sb("zero", [P, 1024])
        ident = sb("ident", [P, P])
        stats, mv = sb("stats", [P, 12]), sb("mv", [P, 2])
        var, rstd, minus_half = sb("var", [P, 1]), sb("rstd", [P, 1]), sb("minus_half", [P, 1])
        ps_t = [pb(f"ps_t{h}", [P, 512]) for h in range(2)]
        ps = [[pb(f"ps{h}{k}", [P, W]) for k in range(3)] for h in range(2)]
        pad_zero, x_loaded, zero_ready, zeros_stored = sem("pad_zero"), sem("x_loaded"), sem("zero_ready"), sem("zeros_stored")
        consts = sem("consts")
        var_ready, rstd_ready = sem("var_ready"), sem("rstd_ready")
        xn_ready = [sem(f"xn_ready{u}") for u in range(3)]
        xn_ready_dma = [sem(f"xn_ready_dma{u}") for u in range(3)]
        xn_used = [sem(f"xn_used{u}") for u in range(3)]
        xn_stored = [sem(f"xn_stored{u}") for u in range(3)]
        t_ready = [sem(f"t_ready{h}") for h in range(2)]
        t_used = [sem(f"t_used{h}") for h in range(2)]
        xnT_ready = sem("xnT_ready")
        w_loaded = [sem(f"w_loaded{h}") for h in range(2)]
        w_used = [sem(f"w_used{h}") for h in range(2)]
        ps_ready = [[sem(f"ps_ready{h}{k}") for k in range(3)] for h in range(2)]
        ps_used = [[sem(f"ps_used{h}{k}") for k in range(3)] for h in range(2)]
        stage_ready = [sem(f"stage_ready{h}") for h in range(2)]
        stage_stored = [sem(f"stage_stored{h}") for h in range(2)]
        rows_out = sem("rows_out")
        block = ctx.enter_context(nc.Block())

        @block.sync
        def _(sp):
            sp.dma_start(x[0:N_META, 0, :], meta).then_inc(x_loaded, 16)
            sp.dma_start(x[N_META:P, 0, :], xp[0:first, :]).then_inc(x_loaded, 16)
            sp.dma_start(x[:, 1:NB - 1, :], xp[first:SEQ - last, :].rearrange("(b p) d -> p b d", p=P)).then_inc(x_loaded, 16)
            sp.wait_ge(pad_zero, 1)
            sp.dma_start(x[0:last, NB - 1, :], xp[SEQ - last:SEQ, :]).then_inc(x_loaded, 16)
            sp.dma_start(x[last:last + N_SAMPLE, NB - 1, :], xs).then_inc(x_loaded, 16)
            sp.dma_start(gain[:, :], io["emb_ln_g"].partition_broadcast(P)).then_inc(x_loaded, 16)
            sp.dma_start(shift[:, :], io["emb_ln_b"].partition_broadcast(P)).then_inc(x_loaded, 16)
            sp.wait_ge(zero_ready, 1)
            n_pad = MIX_ROWS - ROWS
            sp.dma_start(xn_scr[ROWS:MIX_ROWS, :], zero[0:n_pad, :]).then_inc(zeros_stored, 16)
            for c in range(0, IN_WIDTH, 512):
                sp.dma_start(proj[ROWS:MIX_ROWS, c:c + 512], zero[0:n_pad, 0:512]).then_inc(zeros_stored, 16)
            for name in ("o_sb", "o_hg"):
                sp.dma_start(scr[name][N_ROWS:MIX_ROWS, :], zero[0:MIX_ROWS - N_ROWS, 0:512]).then_inc(zeros_stored, 16)
            with sp.Fori(0, NB // 3) as i:
                for u in range(3):
                    sp.wait_ge(xn_ready_dma[u], 1)
                    sp.sem_inc(xn_ready_dma[u], -1)
                    sp.dma_start(xn_scr[bass.ds((3 * i + u) * P, P), :], xn[u][:, :]).then_inc(xn_stored[u], 16)
            with sp.Fori(0, IN_WIDTH // (2 * W)) as g:
                for h in range(2):
                    sp.wait_ge(w_used[h], 1)
                    sp.sem_inc(w_used[h], -1)
                    sp.dma_start(w[h][:, :, :], w_in[:, :, bass.ds(g * 2 * W + h * W, W)]).then_inc(w_loaded[h], 16)
            sp.wait_ge(zeros_stored, 16 * (1 + 7 + 2))
            sp.wait_ge(rows_out, 2)
            outs = [("k_prompt", K_SB, 0, N_PROMPT), ("v_prompt", V_SB, 0, N_PROMPT),
                    ("k_sample", K_SB, SAMPLE0, N_SAMPLE), ("v_sample", V_SB, SAMPLE0, N_SAMPLE)]
            for name, c0, r0, n in outs:
                sp.dma_start(io[name], proj[r0:r0 + n, c0:c0 + SB_WIDTH]).then_inc(rows_out, 16)
            sp.wait_ge(rows_out, 2 + 16 * len(outs))

        @block.gpsimd
        def _(pool):
            nc.gpsimd.memset(x[:, NB - 1, :], 0.0).then_inc(pad_zero, 1)
            nc.gpsimd.memset(zero[:, :], 0.0).then_inc(zero_ready, 1)
            nc.gpsimd.memset(minus_half[:, :], -0.5)
            identity_matrix(nc, pool, ident[:, :])
            pool.drain().then_inc(consts, 1)
            with pool.Fori(0, NB) as i:
                pool.wait_ge(var_ready, 1)
                pool.sem_inc(var_ready, -1)
                nc.gpsimd.tensor_tensor(rstd[:, :], var[:, :], minus_half[:, :], ALU.pow).then_inc(rstd_ready, 1)

        @block.vector
        def _(dve):
            for u in range(3):
                dve.sem_inc(xn_used[u], 1)
                dve.sem_inc(xn_stored[u], 16)
            dve.wait_ge(x_loaded, 16 * 7)
            with dve.Fori(0, NB // 3) as i:
                for u in range(3):
                    xb = x[:, bass.ds(3 * i + u, 1), :].rearrange("p b d -> p (b d)")
                    layer_norm_stats(nc, dve, stats, mv[:, :], xb)
                    nc.vector.tensor_scalar(var[:, :], mv[:, 1:2], EPS, None, ALU.add).then_inc(var_ready, 1)
                    dve.wait_ge(xn_used[u], 1)
                    dve.sem_inc(xn_used[u], -1)
                    dve.wait_ge(xn_stored[u], 16)
                    dve.sem_inc(xn_stored[u], -16)
                    dve.wait_ge(rstd_ready, 1)
                    dve.sem_inc(rstd_ready, -1)
                    normalise(nc, dve, xn[u][:, :], xb, mv[:, 0:1], rstd[:, :], gain[:, :], shift[:, :]).then_inc(xn_ready[u], 1)
                    dve.drain().then_inc(xn_ready_dma[u], 1)
            dve.sem_inc(stage_stored[1], 16)
            with dve.Fori(0, IN_WIDTH // (2 * W)) as g:
                dve.wait_ge(stage_stored[1], 16)
                dve.sem_inc(stage_stored[1], -16)
                for b in range(NB):
                    dve.wait_ge(ps_ready[1][b % 3], 1)
                    dve.sem_inc(ps_ready[1][b % 3], -1)
                    nc.vector.tensor_copy(stage[1][:, b, :], ps[1][b % 3][:, :]).then_inc(ps_used[1][b % 3], 1)
                dve.drain().then_inc(stage_ready[1], 1)

        @block.scalar
        def _(act):
            with act.Fori(0, NB) as i:
                for h in range(2):
                    act.wait_ge(t_ready[h], 1)
                    act.sem_inc(t_ready[h], -1)
                    nc.scalar.copy(xnT[:, 4 * h:4 * h + 4, bass.ds(i * P, P)],
                                   ps_t[h][:, :].rearrange("p (c t) -> p c t", c=4)).then_inc(t_used[h], 1)
            act.drain().then_inc(xnT_ready, 1)
            act.sem_inc(stage_stored[0], 16)
            with act.Fori(0, IN_WIDTH // (2 * W)) as g:
                act.wait_ge(stage_stored[0], 16)
                act.sem_inc(stage_stored[0], -16)
                for b in range(NB):
                    act.wait_ge(ps_ready[0][b % 3], 1)
                    act.sem_inc(ps_ready[0][b % 3], -1)
                    nc.scalar.copy(stage[0][:, b, :], ps[0][b % 3][:, :]).then_inc(ps_used[0][b % 3], 1)
                act.drain()
                act.dma_start(proj[0:ROWS, bass.ds(g * 2 * W, W)].rearrange("(b p) c -> p b c", p=P),
                              stage[0][:, :, :]).then_inc(stage_stored[0], 16)
                act.wait_ge(stage_ready[1], 1)
                act.sem_inc(stage_ready[1], -1)
                act.dma_start(proj[0:ROWS, bass.ds(g * 2 * W + W, W)].rearrange("(b p) c -> p b c", p=P),
                              stage[1][:, :, :]).then_inc(stage_stored[1], 16)
            for h in range(2):
                act.wait_ge(stage_stored[h], 16)
                act.sem_inc(rows_out, 1)

        @block.tensor
        def _(pe):
            pe.wait_ge(consts, 1)
            for h in range(2):
                pe.sem_inc(t_used[h], 1)
                pe.sem_inc(w_used[h], 1)
                for k in range(3):
                    pe.sem_inc(ps_used[h][k], 1)
            with pe.Fori(0, NB // 3) as i:
                for u in range(3):
                    pe.wait_ge(xn_ready[u], 1)
                    pe.sem_inc(xn_ready[u], -1)
                    for h in range(2):
                        pe.wait_ge(t_used[h], 1)
                        pe.sem_inc(t_used[h], -1)
                        for c in range(4):
                            ch = 4 * h + c
                            ins = nc.tensor.transpose(ps_t[h][:, c * P:(c + 1) * P], xn[u][:, ch * P:(ch + 1) * P], ident[:, :])
                        ins.then_inc(t_ready[h], 1)
                    pe.drain().then_inc(xn_used[u], 1)
            pe.wait_ge(xnT_ready, 1)
            with pe.Fori(0, IN_WIDTH // (2 * W)) as g:
                for h in range(2):
                    pe.wait_ge(w_loaded[h], 16)
                    pe.sem_inc(w_loaded[h], -16)
                    for b in range(NB):
                        pe.wait_ge(ps_used[h][b % 3], 1)
                        pe.sem_inc(ps_used[h][b % 3], -1)
                        for c in range(DC):
                            ins = nc.tensor.matmul(ps[h][b % 3][:, :], xnT[:, c, b * P:(b + 1) * P], w[h][:, c, :],
                                                   start=(c == 0), stop=(c == DC - 1))
                        ins.then_inc(ps_ready[h][b % 3], 1)
                    pe.drain().then_inc(w_used[h], 1)


def suffix_matrices(nc, pool, incl, strict):
    nc.gpsimd.memset(incl, 1.0)
    nc.gpsimd.memset(strict, 1.0)
    pool.drain()
    nc.gpsimd.affine_select(out=incl, in_=incl, compare_op=ALU.is_ge, fill=0.0, base=0,
                            pattern=[[-1, P]], channel_multiplier=1)
    nc.gpsimd.affine_select(out=strict, in_=strict, compare_op=ALU.is_gt, fill=0.0, base=0,
                            pattern=[[1, P]], channel_multiplier=-1)


def sb_prompt(nc, io, scr):
    proj, o_sb = scr["proj"], scr["o_sb"]
    CB = 3
    CW = CB * P
    BUF = 4
    tiles = [(c, kb, s) for c in range(NB // CB) for kb in range(CB * c + CB - 1, -1, -1) for s in range(2)]
    NT = len(tiles)

    def cols(n):
        c, kb, s = tiles[n]
        return max(kb - CB * c, 0) * P

    def diagonal(n):
        c, kb, s = tiles[n]
        return kb >= CB * c

    def first_of_chunk(n):
        c, kb, s = tiles[n]
        return kb == CB * c + CB - 1

    with ExitStack() as ctx:
        sb = lambda n, s, d=F32: ctx.enter_context(nc.sbuf_tensor("sp_" + n, s, d))
        pb = lambda n, s: ctx.enter_context(nc.psum_tensor("sp_" + n, s, F32))
        sem = ctx.enter_context(stage_semaphores(nc, "sp_"))
        q_nat, k_nat, v = sb("q_nat", [P, NB, P]), sb("k_nat", [P, NB, P]), sb("v", [P, NB, P])
        qT, kT = sb("qT", [P, ROWS]), sb("kT", [P, ROWS])
        o = sb("o", [P, NB, P])
        bias, bias_pair = sb("bias", [P, SB_HEADS]), sb("bias_pair", [P, 2])
        z = [sb(f"z{k}", [P, CW]) for k in range(BUF)]
        ez = [sb(f"ez{k}", [P, CW]) for k in range(BUF)]
        soft = [sb(f"soft{k}", [P, CW]) for k in range(BUF)]
        wt = [sb(f"wt{k}", [P, CW]) for k in range(BUF)]
        ident, incl, strict = sb("ident", [P, P]), sb("incl", [P, P]), sb("strict", [P, P])
        seen, unseen = sb("seen", [P, P]), sb("unseen", [P, P])
        ps_s = [pb(f"ps_s{k}", [P, 512]) for k in range(BUF)]
        run = [pb(f"run{s}", [P, 512]) for s in range(2)]
        ps_o = [pb(f"ps_o{s}", [P, 512]) for s in range(2)]
        bias_loaded, consts = sem("bias_loaded"), sem("consts")
        qk_loaded, qk_used, v_loaded, v_used = sem("qk_loaded"), sem("qk_used"), sem("v_loaded"), sem("v_used")
        t_ready, t_used = [sem(f"t_ready{k}") for k in range(2)], [sem(f"t_used{k}") for k in range(2)]
        qkT_ready, qkT_used = sem("qkT_ready"), sem("qkT_used")
        each = lambda n: [sem(f"{n}{k}") for k in range(BUF)]
        s_ready, s_used = each("s_ready"), each("s_used")
        capped, log_ready, soft_ready, soft_used = each("capped"), each("log_ready"), each("soft_ready"), each("soft_used")
        x_ready, w_ready, w_used = each("x_ready"), each("w_ready"), each("w_used")
        run_ready, run_read = [sem(f"run_ready{s}") for s in range(2)], [sem(f"run_read{s}") for s in range(2)]
        o_ready, o_used = [sem(f"o_ready{s}") for s in range(2)], [sem(f"o_used{s}") for s in range(2)]
        out_ready, out_stored = sem("out_ready"), sem("out_stored")
        block = ctx.enter_context(nc.Block())

        @block.sync
        def _(sp):
            sp.dma_start(bias[:, :], io["sb_bias"][0].partition_broadcast(P)).then_inc(bias_loaded, 16)

            def rows(c0, pair):
                return proj[0:ROWS, bass.ds(pair * P + c0, P)].rearrange("(b p) c -> p b c", p=P)

            with sp.Fori(0, SB_HEADS // 2) as pair:
                sp.wait_ge(qk_used, 1)
                sp.sem_inc(qk_used, -1)
                sp.dma_start(q_nat[:, :, :], rows(Q_SB, pair)).then_inc(qk_loaded, 16)
                sp.dma_start(k_nat[:, :, :], rows(K_SB, pair)).then_inc(qk_loaded, 16)
                sp.wait_ge(v_used, 1)
                sp.sem_inc(v_used, -1)
                sp.dma_start(v[:, :, :], rows(V_SB, pair)).then_inc(v_loaded, 16)
                sp.wait_ge(out_ready, 1)
                sp.sem_inc(out_ready, -1)
                full = (NB - 1) * P
                sp.dma_start(o_sb[0:full, bass.ds(pair * P, P)].rearrange("(b p) c -> p b c", p=P),
                             o[:, 0:NB - 1, :]).then_inc(out_stored, 16)
                sp.dma_start(o_sb[full:N_PROMPT, bass.ds(pair * P, P)], o[0:N_PROMPT - full, NB - 1, :]).then_inc(out_stored, 16)
            sp.wait_ge(out_stored, 32)

        @block.gpsimd
        def _(pool):
            identity_matrix(nc, pool, ident[:, :])
            suffix_matrices(nc, pool, incl[:, :], strict[:, :])
            nc.gpsimd.memset(seen[:, :], 1.0)
            nc.gpsimd.memset(unseen[:, :], 0.0)
            pool.drain()
            for m, fill in ((seen, 0.0), (unseen, LOWEST)):
                nc.gpsimd.affine_select(out=m[:, :], in_=m[:, :], compare_op=ALU.is_gt, fill=fill, base=0,
                                        pattern=[[1, P]], channel_multiplier=-1)
            pool.drain().then_inc(consts, 2)

        @block.tensor
        def _(pe):
            pe.wait_ge(consts, 1)
            for k in range(BUF):
                pe.sem_inc(s_used[k], 1)
            for s in range(2):
                pe.sem_inc(run_read[s], 1)
                pe.sem_inc(o_used[s], 1)
            for k in range(2):
                pe.sem_inc(t_used[k], 1)

            def scores(n):
                c, kb, s = tiles[n]
                k, lo, d0 = n % BUF, cols(n), s * SB_DIM
                pe.wait_ge(s_used[k], 1)
                pe.sem_inc(s_used[k], -1)
                nc.tensor.matmul(ps_s[k][:, lo:CW], kT[d0:d0 + SB_DIM, kb * P:(kb + 1) * P],
                                 qT[d0:d0 + SB_DIM, c * CW + lo:(c + 1) * CW], start=True, stop=True).then_inc(s_ready[k], 1)

            def own_block(n):
                k, s, lo = n % BUF, tiles[n][2], cols(n)
                pe.wait_ge(soft_ready[k], 1)
                pe.sem_inc(soft_ready[k], -1)
                if first_of_chunk(n):
                    pe.wait_ge(run_read[s], 1)
                    pe.sem_inc(run_read[s], -1)
                nc.tensor.matmul(run[s][:, lo:CW], incl[:, :], soft[k][:, lo:CW], start=first_of_chunk(n), stop=True,
                                 skip_group_check=True).then_inc(run_ready[s], 1)

            def carry(n):
                c, kb, s = tiles[n]
                k, lo = n % BUF, cols(n)
                if kb > 0:
                    pe.wait_ge(run_read[s], 1)
                    pe.sem_inc(run_read[s], -1)
                    nc.tensor.matmul(run[s][:, lo:CW], strict[:, :], soft[k][:, lo:CW], start=False, stop=True,
                                     skip_group_check=True).then_inc(soft_used[k], 1)
                else:
                    pe.sem_inc(soft_used[k], 1)

            def values(n):
                c, kb, s = tiles[n]
                k, lo, d0 = n % BUF, cols(n), s * SB_DIM
                pe.wait_ge(w_ready[k], 1)
                pe.sem_inc(w_ready[k], -1)
                if first_of_chunk(n):
                    pe.wait_ge(o_used[s], 1)
                    pe.sem_inc(o_used[s], -1)
                for q in range(lo // P, CB):
                    ins = nc.tensor.matmul(ps_o[s][:, q * SB_DIM:(q + 1) * SB_DIM], wt[k][:, q * P:(q + 1) * P],
                                           v[:, kb, d0:d0 + SB_DIM], start=first_of_chunk(n), stop=True,
                                           skip_group_check=True)
                ins.then_inc(w_used[k], 1)
                if kb == 0:
                    pe.drain().then_inc(o_ready[s], 1)

            with pe.Fori(0, SB_HEADS // 2) as pair:
                pe.wait_ge(qk_loaded, 32)
                pe.sem_inc(qk_loaded, -32)
                for m, src in ((0, q_nat), (1, k_nat)):
                    for g in range(0, NB, BUF):
                        k = (m * 3 + g // BUF) % 2
                        bank = ps_s[k]
                        pe.wait_ge(t_used[k], 1)
                        pe.sem_inc(t_used[k], -1)
                        for b in range(g, min(g + BUF, NB)):
                            ins = nc.tensor.transpose(bank[:, (b - g) * P:(b - g + 1) * P], src[:, b, :], ident[:, :])
                        ins.then_inc(t_ready[k], 1)
                pe.drain().then_inc(qk_used, 1)
                pe.wait_ge(qkT_ready, 1)
                pe.sem_inc(qkT_ready, -1)
                scores(0)
                scores(1)
                pe.wait_ge(v_loaded, 16)
                pe.sem_inc(v_loaded, -16)
                for n in range(NT + 2):
                    if n + 2 < NT:
                        scores(n + 2)
                    if n < NT:
                        own_block(n)
                    if 1 <= n <= NT:
                        carry(n - 1)
                    if n >= 2:
                        values(n - 2)
                pe.drain().then_inc(v_used, 1)
                for s in range(2):
                    pe.sem_inc(qkT_used, 1)

        @block.vector
        def _(dve):
            dve.wait_ge(bias_loaded, 16)
            dve.wait_ge(consts, 1)
            for k in range(BUF):
                dve.sem_inc(soft_used[k], 1)
                dve.sem_inc(w_used[k], 1)
            dve.sem_inc(qk_used, 1)
            dve.sem_inc(v_used, 1)
            dve.sem_inc(out_stored, 32)

            def logits(n):
                k, lo, s = n % BUF, cols(n), tiles[n][2]
                dve.wait_ge(s_ready[k], 1)
                dve.sem_inc(s_ready[k], -1)
                nc.vector.tensor_scalar(z[k][:, lo:], ps_s[k][:, lo:CW], SB_SCALE, bias_pair[:, s:s + 1],
                                        ALU.mult, ALU.add).then_inc(s_used[k], 1)
                dve.drain()
                nc.vector.tensor_scalar(ez[k][:, lo:], z[k][:, lo:], Z_CAP, None, ALU.min).then_inc(capped[k], 1)

            def softplus(n):
                k, lo = n % BUF, cols(n)
                dve.wait_ge(log_ready[k], 1)
                dve.sem_inc(log_ready[k], -1)
                dve.wait_ge(soft_used[k], 1)
                dve.sem_inc(soft_used[k], -1)
                nc.vector.tensor_tensor(soft[k][:, lo:], ez[k][:, lo:], z[k][:, lo:], ALU.max)
                if diagonal(n):
                    dve.drain()
                    nc.vector.tensor_tensor(soft[k][:, lo:lo + P], soft[k][:, lo:lo + P], seen[:, :], ALU.mult)
                dve.drain().then_inc(soft_ready[k], 1)

            def exponents(n):
                k, lo, s = n % BUF, cols(n), tiles[n][2]
                dve.wait_ge(run_ready[s], 1)
                dve.sem_inc(run_ready[s], -1)
                dve.wait_ge(w_used[k], 1)
                dve.sem_inc(w_used[k], -1)
                nc.vector.tensor_tensor(wt[k][:, lo:], z[k][:, lo:], run[s][:, lo:CW], ALU.subtract).then_inc(run_read[s], 1)
                if diagonal(n):
                    dve.drain()
                    nc.vector.tensor_tensor(wt[k][:, lo:lo + P], wt[k][:, lo:lo + P], unseen[:, :], ALU.add)
                dve.drain().then_inc(x_ready[k], 1)

            def output(n):
                c, kb, s = tiles[n]
                dve.wait_ge(o_ready[s], 1)
                dve.sem_inc(o_ready[s], -1)
                nc.vector.tensor_copy(o[:, CB * c:CB * (c + 1), s * SB_DIM:(s + 1) * SB_DIM],
                                      ps_o[s][:, 0:CB * SB_DIM].rearrange("p (b d) -> p b d", b=CB)).then_inc(o_used[s], 1)

            with dve.Fori(0, SB_HEADS // 2) as pair:
                nc.vector.tensor_copy(bias_pair[:, :], bias[:, bass.ds(2 * pair, 2)])
                dve.wait_ge(out_stored, 32)
                dve.sem_inc(out_stored, -32)
                dve.drain()
                logits(0)
                logits(1)
                softplus(0)
                for n in range(NT + 3):
                    if n + 2 < NT:
                        logits(n + 2)
                    if n + 1 < NT:
                        softplus(n + 1)
                    if n < NT:
                        exponents(n)
                    if n >= 3 and tiles[n - 3][1] == 0:
                        output(n - 3)
                dve.drain().then_inc(out_ready, 1)

        @block.scalar
        def _(act):
            act.preload_act_table_set("natural_log_exp_and_others")
            act.sem_inc(qkT_used, 2)

            def softlog(n):
                k, lo = n % BUF, cols(n)
                act.wait_ge(capped[k], 1)
                act.sem_inc(capped[k], -1)
                nc.scalar.activation(ez[k][:, lo:], ez[k][:, lo:], ACT.Exp)
                act.drain()
                nc.scalar.activation(ez[k][:, lo:], ez[k][:, lo:], ACT.Ln, bias=1.0).then_inc(log_ready[k], 1)

            with act.Fori(0, SB_HEADS // 2) as pair:
                act.wait_ge(qkT_used, 2)
                act.sem_inc(qkT_used, -2)
                for m, dst in ((0, qT), (1, kT)):
                    for g in range(0, NB, BUF):
                        n, k = min(BUF, NB - g), (m * 3 + g // BUF) % 2
                        act.wait_ge(t_ready[k], 1)
                        act.sem_inc(t_ready[k], -1)
                        nc.scalar.copy(dst[:, g * P:(g + n) * P], ps_s[k][:, 0:n * P]).then_inc(t_used[k], 1)
                act.drain().then_inc(qkT_ready, 1)
                softlog(0)
                softlog(1)
                for n in range(NT):
                    if n + 2 < NT:
                        softlog(n + 2)
                    k, lo = n % BUF, cols(n)
                    act.wait_ge(x_ready[k], 1)
                    act.sem_inc(x_ready[k], -1)
                    nc.scalar.activation(wt[k][:, lo:], wt[k][:, lo:], ACT.Exp).then_inc(w_ready[k], 1)


PAGES, PAGE = 32, 128
RUN = 8
GROUP_PAGES = P * RUN // PAGE
GROUPS = PAGES // GROUP_PAGES


def sb_decode(nc, io, scr):
    proj, o_sb = scr["proj"], scr["o_sb"]
    pages = {kv: io["cache_" + kv][0].rearrange("n (r k) h d -> (n r) (k h d)", k=RUN) for kv in "kv"}
    RW = RUN * SB_WIDTH
    PR = PAGE // RUN
    NZ = GROUPS * SB_HEADS * RUN
    with ExitStack() as ctx:
        sb = lambda n, s, d=F32: ctx.enter_context(nc.sbuf_tensor("sd_" + n, s, d))
        pb = lambda n, s: ctx.enter_context(nc.psum_tensor("sd_" + n, s, F32))
        sem = ctx.enter_context(stage_semaphores(nc, "sd_"))
        k_t = [sb(f"k{g}", [P, RW]) for g in range(GROUPS)]
        v_t = [sb(f"v{g}", [P, RW]) for g in range(GROUPS)]
        prod = sb("prod", [P, RW])
        q_all = sb("q_all", [P, N_SAMPLE, SB_WIDTH])
        bias8, bias = sb("bias8", [P, SB_HEADS]), sb("bias", [P, GROUPS, SB_HEADS, RUN])
        NC = N_SAMPLE * GROUPS
        page = sb("page", [P, NC * GROUP_PAGES], I32)
        own = sb("own", [P, NC, GROUP_PAGES])
        page_f, row_f, part_f = sb("page_f", [P, NC, GROUP_PAGES]), sb("row_f", [P, NC]), sb("part_f", [P, 1])
        part = sb("part", [P, 1], I32)
        rows, rows_now = sb("rows", [P, N_SAMPLE * GROUPS], I32), sb("rows_now", [P, 2 * GROUPS], I32)
        shape = [P, GROUPS, SB_HEADS, RUN]
        z, ez, soft, scan, keep, x, w = (sb(n, shape) for n in ("z", "ez", "soft", "scan", "keep", "x", "w"))
        later = sb("later", [P, GROUPS, SB_HEADS])
        after = sb("after", [P, GROUPS, SB_HEADS])
        later_only, ones = sb("later_only", [P, P]), sb("ones", [P, P])
        o = sb("o", [SB_HEADS, SB_WIDTH])
        ps_after = pb("ps_after", [P, 512])
        ps_o = pb("ps_o", [P, 512])
        setup, page_loaded, rows_ready, consts = sem("setup"), sem("page_loaded"), sem("rows_ready"), sem("consts")
        row_picked = sem("row_picked")
        k_loaded, k_used = [sem(f"k_loaded{g}") for g in range(GROUPS)], [sem(f"k_used{g}") for g in range(GROUPS)]
        v_loaded, v_used = [sem(f"v_loaded{g}") for g in range(GROUPS)], [sem(f"v_used{g}") for g in range(GROUPS)]
        capped, log_ready, sums_ready, after_ready = sem("capped"), sem("log_ready"), sem("sums_ready"), sem("after_ready")
        x_ready, w_ready, w_used = sem("x_ready"), sem("w_ready"), sem("w_used")
        o_ready, o_copied, o_stored, rows_stored = (sem(n) for n in ("o_ready", "o_copied", "o_stored", "rows_stored"))
        block = ctx.enter_context(nc.Block())

        @block.sync
        def _(sp):
            sp.dma_start(page[:, :], io["page_table"].rearrange("b n -> (b n)").partition_broadcast(P)).then_inc(page_loaded, 16)
            sp.dma_start(bias8[:, :], io["sb_bias"][0].partition_broadcast(P)).then_inc(setup, 16)
            for b in range(N_SAMPLE):
                sp.dma_start(q_all[:, b, :], proj[SAMPLE0 + b, Q_SB:Q_SB + SB_WIDTH].partition_broadcast(P)).then_inc(setup, 16)
            with sp.Fori(0, N_SAMPLE) as b:
                sp.wait_ge(o_copied, 1)
                sp.sem_inc(o_copied, -1)
                sp.dma_start(scr["o_heads"][bass.ds(b * SB_HEADS, SB_HEADS), :], o[:, :]).then_inc(o_stored, 16)
            sp.wait_ge(o_stored, 16)
            for h in range(SB_HEADS):
                c = slice(h * SB_DIM, (h + 1) * SB_DIM)
                sp.dma_start(o_sb[SAMPLE0:N_ROWS, c], scr["o_heads"][h:N_SAMPLE * SB_HEADS:SB_HEADS, c]).then_inc(rows_stored, 16)
            sp.wait_ge(rows_stored, 16 * SB_HEADS)

        @block.gpsimd
        def _(pool):
            nc.gpsimd.iota(part[:, :], pattern=[[0, 1]], base=0, channel_multiplier=1)
            nc.gpsimd.memset(ones[:, :], 1.0)
            nc.gpsimd.memset(later_only[:, :], 1.0)
            nc.gpsimd.memset(own[:, :, :], 1.0)
            nc.gpsimd.memset(keep[:, :, :, :], 1.0)
            pool.drain()
            nc.gpsimd.memset(keep[:, :, :, 0:1], 0.0)
            nc.gpsimd.affine_select(out=later_only[:, :], in_=later_only[:, :], compare_op=ALU.is_gt, fill=0.0,
                                    base=0, pattern=[[-1, P]], channel_multiplier=1)
            nc.gpsimd.affine_select(out=own[:, :, :], in_=own[:, :, :], compare_op=ALU.is_ge, fill=0.0, base=0,
                                    pattern=[[0, NC], [-PR, GROUP_PAGES]], channel_multiplier=1)
            pool.drain()
            nc.gpsimd.affine_select(out=own[:, :, :], in_=own[:, :, :], compare_op=ALU.is_ge, fill=0.0, base=PR - 1,
                                    pattern=[[0, NC], [PR, GROUP_PAGES]], channel_multiplier=-1)
            pool.drain().then_inc(consts, 3)
            pool.wait_ge(rows_ready, 1)
            for g in range(GROUPS):
                pool.sem_inc(k_used[g], 1)
                pool.sem_inc(v_used[g], 1)
            with pool.Fori(0, N_SAMPLE) as b:
                for n, (t, src, used, loaded) in enumerate(((k_t, pages["k"], k_used, k_loaded),
                                                            (v_t, pages["v"], v_used, v_loaded))):
                    for g in range(GROUPS):
                        pool.wait_ge(used[g], 1)
                        pool.sem_inc(used[g], -1)
                        c = n * GROUPS + g
                        nc.gpsimd.tensor_copy(rows_now[:, c:c + 1], rows[:, bass.ds(b * GROUPS + g, 1)]).then_inc(row_picked, 1)
                        pool.wait_ge(row_picked, 1)
                        pool.sem_inc(row_picked, -1)
                        pool.indirect_dma_start(t[g][:, :], None, src,
                                                bass.IndirectOffsetOnAxis(ap=rows_now[:, c:c + 1], axis=0)).then_inc(loaded[g], 16)

        @block.vector
        def _(dve):
            dve.wait_ge(consts, 1)
            dve.wait_ge(page_loaded, 16)
            nc.vector.tensor_scalar(part[:, :], part[:, :], PR - 1, None, ALU.bitwise_and)
            nc.vector.tensor_copy(page_f[:, :, :].rearrange("p c j -> p (c j)"), page[:, :])
            dve.drain()
            nc.vector.tensor_copy(part_f[:, :], part[:, :])
            nc.vector.tensor_tensor(page_f[:, :, :], page_f[:, :, :], own[:, :, :], ALU.mult)
            dve.drain()
            nc.vector.tensor_reduce(row_f[:, :], page_f[:, :, :], AX.X, ALU.add)
            dve.drain()
            nc.vector.tensor_scalar(rows[:, :], row_f[:, :], float(PR), part_f[:, :], ALU.mult, ALU.add)
            dve.drain().then_inc(rows_ready, 1)
            dve.wait_ge(setup, 16 * (1 + N_SAMPLE))
            nc.vector.tensor_copy(bias[:, :, :, :], bias8[:, :].rearrange("p (g h k) -> p g h k", g=1, k=1).broadcast_to(shape))
            nc.vector.memset(later[:, GROUPS - 1, :], 0.0)
            dve.drain()
            flat = lambda t: t[:, :, :, :].rearrange("p g h k -> p (g h k)")
            with dve.Fori(0, N_SAMPLE) as b:
                for g in range(GROUPS):
                    dve.wait_ge(k_loaded[g], b * 16 + 16)
                    nc.vector.tensor_tensor(prod[:, :].rearrange("p (k n) -> p k n", k=RUN),
                                            k_t[g][:, :].rearrange("p (k n) -> p k n", k=RUN),
                                            q_all[:, bass.ds(b, 1), :].broadcast_to([P, RUN, SB_WIDTH]),
                                            ALU.mult).then_inc(k_used[g], 1)
                    dve.drain()
                    nc.vector.tensor_reduce(z[:, g, :, :].rearrange("p h k -> p k h"),
                                            prod[:, :].rearrange("p (k h d) -> p k h d", k=RUN, h=SB_HEADS), AX.X, ALU.add)
                    dve.drain()
                nc.vector.scalar_tensor_tensor(out=flat(z), in0=flat(z), scalar=SB_SCALE, in1=flat(bias),
                                               op0=ALU.mult, op1=ALU.add)
                dve.drain()
                nc.vector.tensor_scalar(flat(ez), flat(z), Z_CAP, None, ALU.min).then_inc(capped, 1)
                dve.wait_ge(log_ready, 1)
                dve.sem_inc(log_ready, -1)
                nc.vector.tensor_tensor(flat(soft), flat(ez), flat(z), ALU.max)
                dve.drain()
                nc.vector.tensor_tensor_scan(flat(scan), flat(keep), flat(soft), 0.0, ALU.mult, ALU.add)
                dve.drain()
                total = scan[:, :, :, RUN - 1]
                nc.vector.tensor_copy(later[:, 2, :], total[:, 3, :])
                nc.vector.tensor_tensor(later[:, 1, :], total[:, 3, :], total[:, 2, :], ALU.add)
                dve.drain()
                nc.vector.tensor_tensor(later[:, 0, :], later[:, 1, :], total[:, 1, :], ALU.add)
                dve.drain().then_inc(sums_ready, 1)
                nc.vector.tensor_tensor(flat(x), flat(z), flat(soft), ALU.subtract)
                dve.drain()
                nc.vector.tensor_tensor(flat(x), flat(x), flat(scan), ALU.add)
                dve.wait_ge(after_ready, 1)
                dve.sem_inc(after_ready, -1)
                nc.vector.tensor_tensor(after[:, :, :], total, ps_after[:, 0:GROUPS * SB_HEADS].rearrange("p (g h) -> p g h", g=GROUPS), ALU.add)
                dve.drain()
                nc.vector.tensor_tensor(x[:, :, :, :].rearrange("p g h k -> p (g h) k"), x[:, :, :, :].rearrange("p g h k -> p (g h) k"),
                                        after[:, :, :].rearrange("p g h -> p (g h)").unsqueeze(2).broadcast_to([P, GROUPS * SB_HEADS, RUN]),
                                        ALU.subtract).then_inc(x_ready, 1)

        @block.scalar
        def _(act):
            act.preload_act_table_set("natural_log_exp_and_others")
            act.sem_inc(w_used, 1)
            act.sem_inc(o_stored, 16)
            flat = lambda t: t[:, :, :, :].rearrange("p g h k -> p (g h k)")
            with act.Fori(0, N_SAMPLE) as b:
                act.wait_ge(capped, 1)
                act.sem_inc(capped, -1)
                nc.scalar.activation(flat(ez), flat(ez), ACT.Exp)
                act.drain()
                nc.scalar.activation(flat(ez), flat(ez), ACT.Ln, bias=1.0).then_inc(log_ready, 1)
                act.wait_ge(x_ready, 1)
                act.sem_inc(x_ready, -1)
                act.wait_ge(w_used, 1)
                act.sem_inc(w_used, -1)
                nc.scalar.activation(flat(w), flat(x), ACT.Exp).then_inc(w_ready, 1)
                act.wait_ge(o_ready, 1)
                act.sem_inc(o_ready, -1)
                act.wait_ge(o_stored, 16)
                act.sem_inc(o_stored, -16)
                nc.scalar.copy(o[:, :], ps_o[0:SB_HEADS, :]).then_inc(o_copied, 1)

        @block.tensor
        def _(pe):
            pe.wait_ge(consts, 1)
            NG = GROUPS * SB_HEADS
            with pe.Fori(0, N_SAMPLE) as b:
                pe.wait_ge(sums_ready, 1)
                pe.sem_inc(sums_ready, -1)
                nc.tensor.matmul(ps_after[:, 0:NG], later_only[:, :], scan[:, :, :, RUN - 1].rearrange("p g h -> p (g h)"),
                                 start=True, stop=False)
                nc.tensor.matmul(ps_after[:, 0:NG], ones[:, :], later[:, :, :].rearrange("p g h -> p (g h)"),
                                 start=False, stop=True).then_inc(after_ready, 1)
                pe.wait_ge(w_ready, 1)
                pe.sem_inc(w_ready, -1)
                for g in range(GROUPS):
                    pe.wait_ge(v_loaded[g], b * 16 + 16)
                    for k in range(RUN):
                        ins = nc.tensor.matmul(ps_o[0:SB_HEADS, :], w[:, g, :, k], v_t[g][:, k * SB_WIDTH:(k + 1) * SB_WIDTH],
                                               start=(g == 0 and k == 0), stop=(g == GROUPS - 1 and k == RUN - 1))
                    ins.then_inc(v_used[g], 1)
                pe.drain().then_inc(o_ready, 1)
                pe.sem_inc(w_used, 1)


CHUNK = 26
N_CHUNK = N_PROMPT // CHUNK
TURN = 5
DECAY_CAP = 80.0


MID = CHUNK // 2 - 1
QE, QM, KM, KE = range(4)


def hgrn_gates(nc, io, scr, factors, decay, f_s, k_s, q_s):
    proj = scr["proj"]
    with ExitStack() as ctx:
        sb = lambda n, s, d=F32: ctx.enter_context(nc.sbuf_tensor("hg_" + n, s, d))
        pb = lambda n, s: ctx.enter_context(nc.psum_tensor("hg_" + n, s, F32))
        sem = ctx.enter_context(stage_semaphores(nc, "hg_"))
        f_nat, q_nat = sb("f_nat", [P, NB, P]), sb("q_nat", [P, NB, P])
        sig_f, sig_nf, sig_q = sb("sig_f", [P, ROWS]), sb("sig_nf", [P, ROWS]), sb("sig_q", [P, ROWS])
        G, rel, e_mid, e_neg, e_last = (sb(n, [P, N_PROMPT]) for n in ("G", "rel", "e_mid", "e_neg", "e_last"))
        keep = sb("keep", [P, N_PROMPT])
        lbp, lb, lb1 = sb("lbp", [P, 2, HG_HEADS]), sb("lb", [P, HG_HEADS]), sb("lb1", [P, HG_HEADS])
        lb_h, lb1_h = sb("lb_h", [P, 1]), sb("lb1_h", [P, 1])
        lb_max, lb_sum = sb("lb_max", [P, HG_HEADS]), sb("lb_sum", [P, HG_HEADS])
        lb_rows = sb("lb_rows", [2 * HG_HEADS, P])
        ident = sb("ident", [P, P])
        psw = pb("psw", [P, 1536])
        psq = pb("psq", [P, 1536])
        lb_loaded, lb_t, lb_max_ready, lb_exp, consts = sem("lb_loaded"), sem("lb_t"), sem("lb_max"), sem("lb_exp"), sem("consts")
        nat_loaded, nat_used, t_ready, t_used = sem("nat_loaded"), sem("nat_used"), sem("t_ready"), sem("t_used")
        sig_ready, f_ready, log_ready, sums_ready, exps_ready, head_done = (
            sem(n) for n in ("sig_ready", "f_ready", "log_ready", "sums_ready", "exps_ready", "head_done"))
        block = ctx.enter_context(nc.Block())

        @block.sync
        def _(sp):
            sp.dma_start(lb_rows[:, :], io["lb_param"].rearrange("l (h k) -> (l h) k", h=HG_HEADS)).then_inc(lb_loaded, 16)
            with sp.Fori(0, HG_HEADS) as h:
                sp.wait_ge(nat_used, 1)
                sp.sem_inc(nat_used, -1)
                for t, c0 in ((f_nat, F_HG), (q_nat, Q_HG)):
                    sp.dma_start(t[:, :, :], proj[0:ROWS, bass.ds(h * HG_D + c0, HG_D)].rearrange("(b p) c -> p b c", p=P)).then_inc(nat_loaded, 16)

        @block.gpsimd
        def _(pool):
            identity_matrix(nc, pool, ident[:, :])
            nc.gpsimd.memset(keep[:, :], 1.0)
            pool.drain()
            nc.gpsimd.memset(keep[:, :].rearrange("p (c t) -> p c t", t=CHUNK)[:, :, 0:1], 0.0)
            pool.drain().then_inc(consts, 2)

        @block.tensor
        def _(pe):
            pe.wait_ge(consts, 1)
            pe.wait_ge(lb_loaded, 16)
            nc.tensor.transpose(psw[:, 0:2 * HG_HEADS], lb_rows[:, :], ident[0:2 * HG_HEADS, 0:2 * HG_HEADS]).then_inc(lb_t, 1)
            pe.sem_inc(nat_used, 1)
            with pe.Fori(0, HG_HEADS) as h:
                pe.wait_ge(nat_loaded, 32)
                pe.sem_inc(nat_loaded, -32)
                pe.wait_ge(t_used, 1)
                pe.sem_inc(t_used, -1)
                for dst, src in ((psw, f_nat), (psq, q_nat)):
                    for b in range(NB):
                        ins = nc.tensor.transpose(dst[:, b * P:(b + 1) * P], src[:, b, :], ident[:, :])
                pe.drain().then_inc(t_ready, 1)
                pe.sem_inc(nat_used, 1)

        @block.scalar
        def _(act):
            act.wait_ge(lb_max_ready, 1)
            nc.scalar.activation(lbp[:, :, :], lbp[:, :, :], ACT.Exp).then_inc(lb_exp, 1)
            with act.Fori(0, HG_HEADS) as h:
                act.wait_ge(t_ready, 1)
                act.sem_inc(t_ready, -1)
                act.wait_ge(head_done, 1)
                act.sem_inc(head_done, -1)
                nc.scalar.activation(sig_f[:, :], psw[:, 0:ROWS], ACT.Sigmoid)
                nc.scalar.activation(sig_nf[:, :], psw[:, 0:ROWS], ACT.Sigmoid, scale=-1.0)
                nc.scalar.activation(sig_q[:, :], psq[:, 0:ROWS], ACT.Sigmoid)
                act.drain().then_inc(sig_ready, 1)
                act.wait_ge(f_ready, 1)
                act.sem_inc(f_ready, -1)
                nc.scalar.activation(rel[:, :], sig_f[:, 0:N_PROMPT], ACT.Ln).then_inc(log_ready, 1)
                act.wait_ge(sums_ready, 1)
                act.sem_inc(sums_ready, -1)
                for t in (e_mid, e_neg, e_last):
                    nc.scalar.activation(t[:, :], t[:, :], ACT.Exp)
                nc.scalar.activation(G[:, :], G[:, :], ACT.Exp)
                act.drain().then_inc(exps_ready, 1)

        @block.vector
        def _(dve):
            dve.wait_ge(lb_t, 1)
            nc.vector.tensor_copy(lbp[:, :, :].rearrange("p l h -> p (l h)"), psw[:, 0:2 * HG_HEADS])
            dve.drain()
            dve.sem_inc(t_used, 1)
            dve.sem_inc(head_done, 1)
            nc.vector.tensor_tensor(lb_max[:, :], lbp[:, 0, :], lbp[:, 1, :], ALU.max)
            dve.drain()
            for l in range(2):
                nc.vector.tensor_tensor(lbp[:, l, :], lbp[:, l, :], lb_max[:, :], ALU.subtract)
            dve.drain().then_inc(lb_max_ready, 1)
            dve.wait_ge(lb_exp, 1)
            nc.vector.tensor_tensor(lb_sum[:, :], lbp[:, 0, :], lbp[:, 1, :], ALU.add)
            dve.drain()
            nc.vector.reciprocal(lb_sum[:, :], lb_sum[:, :])
            dve.drain()
            nc.vector.tensor_tensor(lb[:, :], lbp[:, 0, :], lb_sum[:, :], ALU.mult)
            nc.vector.tensor_tensor(lb1[:, :], lbp[:, 1, :], lb_sum[:, :], ALU.mult)
            dve.wait_ge(consts, 1)
            dve.drain()
            chunks = lambda t: t[:, 0:N_PROMPT].rearrange("p (c t) -> p c t", t=CHUNK)
            wide = [P, N_CHUNK, CHUNK]
            with dve.Fori(0, HG_HEADS) as h:
                nc.vector.tensor_copy(lb_h[:, :], lb[:, bass.ds(h, 1)])
                nc.vector.tensor_copy(lb1_h[:, :], lb1[:, bass.ds(h, 1)])
                dve.wait_ge(sig_ready, 1)
                dve.sem_inc(sig_ready, -1)
                dve.drain()
                nc.vector.tensor_scalar(sig_f[:, :], sig_f[:, :], lb1_h[:, :], lb_h[:, :], ALU.mult, ALU.add)
                dve.drain().then_inc(f_ready, 1)
                nc.vector.tensor_scalar(sig_nf[:, :], sig_nf[:, :], lb1_h[:, :], None, ALU.mult)
                nc.vector.scalar_tensor_tensor(out=sig_q[:, :], in0=psq[:, 0:ROWS], scalar=HG_SCALE, in1=sig_q[:, :],
                                               op0=ALU.mult, op1=ALU.mult)
                dve.drain().then_inc(t_used, 1)
                for dst, src in ((f_s, sig_f), (k_s, sig_nf), (q_s, sig_q)):
                    nc.vector.tensor_copy(dst[:, bass.ds(h, 1), :].rearrange("p h b -> p (h b)"), src[:, SAMPLE0:SAMPLE0 + N_SAMPLE])
                dve.wait_ge(log_ready, 1)
                dve.sem_inc(log_ready, -1)
                nc.vector.tensor_tensor_scan(G[:, :], keep[:, :], rel[:, :], 0.0, ALU.mult, ALU.add)
                dve.drain()
                Gc = chunks(G)
                nc.vector.tensor_tensor(chunks(rel), Gc, Gc[:, :, MID:MID + 1].broadcast_to(wide), ALU.subtract)
                nc.vector.tensor_tensor(chunks(e_last), Gc[:, :, CHUNK - 1:CHUNK].broadcast_to(wide), Gc, ALU.subtract)
                dve.drain()
                nc.vector.tensor_scalar(e_mid[:, :], rel[:, :], DECAY_CAP, None, ALU.min)
                nc.vector.tensor_scalar(e_neg[:, :], rel[:, :], -1.0, DECAY_CAP, ALU.mult, ALU.min)
                dve.drain().then_inc(sums_ready, 1)
                dve.wait_ge(exps_ready, 1)
                dve.sem_inc(exps_ready, -1)
                for kind, base, e in ((QE, sig_q, G), (QM, sig_q, e_mid), (KM, sig_nf, e_neg), (KE, sig_nf, e_last)):
                    nc.vector.tensor_tensor(factors[:, :, kind, bass.ds(h, 1), :].rearrange("p c h t -> p c (h t)"),
                                            chunks(base), chunks(e), ALU.mult)
                nc.vector.tensor_copy(decay[:, :, bass.ds(h, 1)], chunks(G)[:, :, CHUNK - 1:CHUNK])
                dve.drain().then_inc(head_done, 1)



def hgrn_steps(nc, io, scr, factors, decay):
    proj, o_hg = scr["proj"], scr["o_hg"]
    with ExitStack() as ctx:
        sb = lambda n, s, d=F32: ctx.enter_context(nc.sbuf_tensor("hs_" + n, s, d))
        pb = lambda n, s: ctx.enter_context(nc.psum_tensor("hs_" + n, s, F32))
        sem = ctx.enter_context(stage_semaphores(nc, "hs_"))
        ident = sb("ident", [P, P])
        causal = sb("causal", [CHUNK, HG_HEADS, CHUNK])
        step = [sb(f"step{u}", [P, 4, HG_HEADS, CHUNK]) for u in range(TURN)]
        step_decay = [sb(f"step_decay{u}", [P, HG_HEADS]) for u in range(TURN)]
        v = [sb(f"v{u}", [CHUNK, HG_WIDTH]) for u in range(TURN)]
        kn = [sb(f"kn{u}", [CHUNK, HG_WIDTH]) for u in range(TURN)]
        score = [sb(f"score{u}", [CHUNK, HG_HEADS, CHUNK]) for u in range(TURN)]
        oT = sb("oT", [P, HG_HEADS, NB * P])
        o = [sb(f"o{j}", [P, HG_WIDTH]) for j in range(2)]
        S = [sb(f"S{u}", [P, HG_HEADS, HG_D]) for u in range(TURN)]
        ps_k, ps_a, ps_kv, ps_o = ([pb(f"{n}{j}", [P, 512]) for j in range(2)] for n in ("ps_k", "ps_a", "ps_kv", "ps_o"))
        each = lambda n, k=TURN: [sem(f"{n}{u}") for u in range(k)]
        consts, state_out, pad_ready = sem("consts"), sem("state_out"), sem("pad_ready")
        rows_ready = [sem(f"rows_ready{j}") for j in range(2)]
        v_loaded, v_used, step_ready, step_used, decay_used = each("v_loaded"), each("v_used"), each("step_ready"), each("step_used"), each("decay_used")
        kn_ready, score_ready, s_ready, s_used = each("kn_ready"), each("score_ready"), each("s_ready"), each("s_used")
        oT_done = sem("oT_done")
        o_copied, o_stored = each("o_copied", 2), each("o_stored", 2)
        t_ready, a_ready, kv_ready, o_ready = each("t_ready", 2), each("a_ready", 2), each("kv_ready", 2), each("o_ready", 2)
        t_used, a_used, kv_used, o_used = each("t_used", 2), each("a_used", 2), each("kv_used", 2), each("o_used", 2)
        block = ctx.enter_context(nc.Block())

        @block.sync
        def _(sp):
            with sp.Fori(0, N_CHUNK // TURN) as i:
                for u in range(TURN):
                    sp.wait_ge(v_used[u], 1)
                    sp.sem_inc(v_used[u], -1)
                    sp.dma_start(v[u][:, :], proj[bass.ds((i * TURN + u) * CHUNK, CHUNK), I_HG:I_HG + HG_WIDTH]).then_inc(v_loaded[u], 16)
            for b in range(NB):
                j, rows = b % 2, min(P, N_PROMPT - b * P)
                sp.wait_ge(o_copied[j], b // 2 + 1)
                sp.dma_start(o_hg[b * P:b * P + rows, :], o[j][0:rows, :]).then_inc(o_stored[j], 16)
            for j in range(2):
                sp.wait_ge(o_stored[j], 16 * ((NB + 1 - j) // 2))
            sp.wait_ge(s_ready[0], 1)
            sp.dma_start(io["s_prompt"].rearrange("h k v -> k h v"), S[0][:, :, :]).then_inc(state_out, 16)
            sp.wait_ge(state_out, 16)

        @block.gpsimd
        def _(pool):
            identity_matrix(nc, pool, ident[:, :])
            nc.gpsimd.memset(causal[:, :, :], 1.0)
            pool.drain()
            nc.gpsimd.affine_select(out=causal[:, :, :], in_=causal[:, :, :], compare_op=ALU.is_ge, fill=0.0, base=0,
                                    pattern=[[0, HG_HEADS], [1, CHUNK]], channel_multiplier=-1)
            nc.gpsimd.memset(oT[:, :, N_PROMPT:NB * P], 0.0)
            pool.drain().then_inc(consts, 2)
            pool.sem_inc(pad_ready, 1)
            for u in range(TURN):
                pool.sem_inc(step_used[u], 1)
                pool.sem_inc(decay_used[u], 1)
            with pool.Fori(0, N_CHUNK // TURN) as i:
                for u in range(TURN):
                    pool.wait_ge(step_used[u], 1)
                    pool.sem_inc(step_used[u], -1)
                    nc.gpsimd.tensor_copy(step[u][:, :, :, :].rearrange("p k h t -> p (k h t)"),
                                          factors[:, bass.ds(i * TURN + u, 1), :, :, :].rearrange("p c k h t -> p (c k h t)"))
                    pool.wait_ge(decay_used[u], 1)
                    pool.sem_inc(decay_used[u], -1)
                    nc.gpsimd.tensor_copy(step_decay[u][:, :], decay[:, bass.ds(i * TURN + u, 1), :].rearrange("p c h -> p (c h)"))
                    pool.drain().then_inc(step_ready[u], 2)

        @block.tensor
        def _(pe):
            pe.wait_ge(consts, 1)
            for j in range(2):
                for used in (t_used, a_used, kv_used, o_used):
                    pe.sem_inc(used[j], 1)
            for u in range(TURN):
                pe.sem_inc(v_used[u], 1)

            def within(u):
                j = u % 2
                pe.wait_ge(step_ready[u], 1)
                pe.sem_inc(step_ready[u], -1)
                pe.wait_ge(t_used[j], 1)
                pe.sem_inc(t_used[j], -1)
                for h in range(HG_HEADS):
                    ins = nc.tensor.transpose(ps_k[j][0:CHUNK, h * HG_D:(h + 1) * HG_D], step[u][:, KE, h, :], ident[:, :])
                ins.then_inc(t_ready[j], 1)
                pe.wait_ge(a_used[j], 1)
                pe.sem_inc(a_used[j], -1)
                for h in range(HG_HEADS):
                    ins = nc.tensor.matmul(ps_a[j][0:CHUNK, h * CHUNK:(h + 1) * CHUNK], step[u][:, KM, h, :], step[u][:, QM, h, :],
                                           start=True, stop=True)
                ins.then_inc(a_ready[j], 1)

            def outputs(u):
                j = u % 2
                pe.wait_ge(v_loaded[u], 16)
                pe.sem_inc(v_loaded[u], -16)
                pe.wait_ge(kn_ready[u], 1)
                pe.sem_inc(kn_ready[u], -1)
                pe.wait_ge(kv_used[j], 1)
                pe.sem_inc(kv_used[j], -1)
                for h in range(HG_HEADS):
                    c = slice(h * HG_D, (h + 1) * HG_D)
                    ins = nc.tensor.matmul(ps_kv[j][:, c], kn[u][:, c], v[u][:, c], start=True, stop=True)
                ins.then_inc(kv_ready[j], 1)
                pe.wait_ge(score_ready[u], 1)
                pe.sem_inc(score_ready[u], -1)
                pe.wait_ge(o_used[j], 1)
                pe.sem_inc(o_used[j], -1)
                pe.wait_ge(s_ready[u], 1)
                pe.sem_inc(s_ready[u], -1)
                for h in range(HG_HEADS):
                    c, t = slice(h * HG_D, (h + 1) * HG_D), slice(h * CHUNK, (h + 1) * CHUNK)
                    nc.tensor.matmul(ps_o[j][:, t], v[u][:, c], score[u][:, h, :], start=True, stop=False)
                    ins = nc.tensor.matmul(ps_o[j][:, t], S[u][:, h, :], step[u][:, QE, h, :], start=False, stop=True)
                ins.then_inc(o_ready[j], 1)
                pe.drain().then_inc(v_used[u], 1)
                pe.sem_inc(step_used[u], 1)
                pe.sem_inc(s_used[u], 1)

            with pe.Fori(0, N_CHUNK // TURN) as i:
                within(0)
                for u in range(TURN):
                    if u + 1 < TURN:
                        within(u + 1)
                    outputs(u)
            pe.wait_ge(oT_done, 1)
            for b in range(NB):
                j = b % 2
                if b >= 2:
                    pe.wait_ge(o_copied[j], b // 2)
                else:
                    pe.wait_ge(kv_used[j], 1)
                for h in range(HG_HEADS):
                    ins = nc.tensor.transpose(ps_kv[j][:, h * HG_D:(h + 1) * HG_D], oT[:, h, b * P:(b + 1) * P], ident[:, :])
                ins.then_inc(rows_ready[j], 1)

        @block.scalar
        def _(act):
            with act.Fori(0, N_CHUNK // TURN) as i:
                for u in range(TURN + 1):
                    if u < TURN:
                        j = u % 2
                        act.wait_ge(t_ready[j], 1)
                        act.sem_inc(t_ready[j], -1)
                        nc.scalar.copy(kn[u][:, :], ps_k[j][0:CHUNK, :])
                        act.drain().then_inc(kn_ready[u], 1)
                        act.sem_inc(t_used[j], 1)
                    if u > 0:
                        w = u - 1
                        act.wait_ge(o_ready[w % 2], 1)
                        act.sem_inc(o_ready[w % 2], -1)
                        nc.scalar.copy(oT[:, :, bass.ds((i * TURN + w) * CHUNK, CHUNK)],
                                       ps_o[w % 2][:, 0:HG_HEADS * CHUNK].rearrange("p (h t) -> p h t", h=HG_HEADS)).then_inc(o_used[w % 2], 1)
            act.wait_ge(pad_ready, 1)
            act.drain().then_inc(oT_done, 1)
            for b in range(NB):
                j = b % 2
                act.wait_ge(rows_ready[j], b // 2 + 1)
                if b >= 2:
                    act.wait_ge(o_stored[j], 16 * (b // 2))
                nc.scalar.copy(o[j][:, :], ps_kv[j][:, :]).then_inc(o_copied[j], 1)

        @block.vector
        def _(dve):
            nc.vector.memset(S[0][:, :, :], 0.0)
            for u in range(1, TURN):
                dve.sem_inc(s_used[u], 1)
            dve.wait_ge(consts, 2)
            dve.drain().then_inc(s_ready[0], 1)

            def mask(u):
                j = u % 2
                dve.wait_ge(a_ready[j], 1)
                dve.sem_inc(a_ready[j], -1)
                nc.vector.tensor_tensor(score[u][:, :, :], ps_a[j][0:CHUNK, 0:HG_HEADS * CHUNK].rearrange("p (h t) -> p h t", h=HG_HEADS),
                                        causal[:, :, :], ALU.mult).then_inc(a_used[j], 1)
                dve.drain().then_inc(score_ready[u], 1)

            with dve.Fori(0, N_CHUNK // TURN) as i:
                mask(0)
                for u in range(TURN):
                    if u + 1 < TURN:
                        mask(u + 1)
                    j, n = u % 2, (u + 1) % TURN
                    dve.wait_ge(step_ready[u], 1)
                    dve.sem_inc(step_ready[u], -1)
                    dve.wait_ge(kv_ready[j], 1)
                    dve.sem_inc(kv_ready[j], -1)
                    dve.wait_ge(s_used[n], 1)
                    dve.sem_inc(s_used[n], -1)
                    for h in range(HG_HEADS):
                        ins = nc.vector.scalar_tensor_tensor(out=S[n][:, h, :], in0=S[u][:, h, :], scalar=step_decay[u][:, h:h + 1],
                                                             in1=ps_kv[j][:, h * HG_D:(h + 1) * HG_D], op0=ALU.mult, op1=ALU.add)
                    dve.drain().then_inc(s_ready[n], 1)
                    dve.sem_inc(kv_used[j], 1)
                    dve.sem_inc(decay_used[u], 1)


def hgrn_sample(nc, io, scr, f_s, k_s, q_s):
    proj, o_hg = scr["proj"], scr["o_hg"]
    NS, H = N_SAMPLE, HG_HEADS
    with ExitStack() as ctx:
        sb = lambda n, s, d=F32: ctx.enter_context(nc.sbuf_tensor("hn_" + n, s, d))
        pb = lambda n, s: ctx.enter_context(nc.psum_tensor("hn_" + n, s, F32))
        sem = ctx.enter_context(stage_semaphores(nc, "hn_"))
        ident = sb("ident", [P, P])
        S = sb("S", [P, NS, H, HG_D])
        v = sb("v", [NS, HG_WIDTH])
        k_nat = sb("k_nat", [NS, HG_WIDTH])
        k_own = sb("k_own", [NS, NS, HG_WIDTH])
        oT, o = sb("oT", [P, H, NS]), sb("o", [NS, HG_WIDTH])
        ps_k, ps_oT, ps_o = pb("ps_k", [P, 512]), pb("ps_oT", [P, 512]), pb("ps_o", [P, 512])
        ps_kv = [pb(f"ps_kv{j}", [P, 512]) for j in range(2)]
        loaded, consts, k_ready, k_copied, own_ready = (sem(n) for n in ("loaded", "consts", "k_ready", "k_copied", "own_ready"))
        kv_ready, kv_used = [sem(f"kv_ready{j}") for j in range(2)], [sem(f"kv_used{j}") for j in range(2)]
        s_ready, oT_ready, oT_copied, o_ready, o_copied, stored = (
            sem(n) for n in ("s_ready", "oT_ready", "oT_copied", "o_ready", "o_copied", "stored"))
        block = ctx.enter_context(nc.Block())

        @block.sync
        def _(sp):
            sp.dma_start(S[:, :, :, :], io["state_hgrn"][0].rearrange("b h k v -> k b h v")).then_inc(loaded, 16)
            sp.dma_start(v[:, :], proj[SAMPLE0:SAMPLE0 + NS, I_HG:I_HG + HG_WIDTH]).then_inc(loaded, 16)
            sp.wait_ge(s_ready, NS)
            sp.dma_start(io["s_sample"].rearrange("b h k v -> k b h v"), S[:, :, :, :]).then_inc(stored, 16)
            sp.wait_ge(o_copied, 1)
            sp.dma_start(o_hg[SAMPLE0:SAMPLE0 + NS, :], o[:, :]).then_inc(stored, 16)
            sp.wait_ge(stored, 32)

        @block.gpsimd
        def _(pool):
            identity_matrix(nc, pool, ident[:, :])
            pool.drain().then_inc(consts, 2)

        @block.tensor
        def _(pe):
            pe.wait_ge(consts, 1)
            for h in range(H):
                ins = nc.tensor.transpose(ps_k[0:NS, h * HG_D:(h + 1) * HG_D], k_s[:, h, :], ident[:, :])
            ins.then_inc(k_ready, 1)
            pe.wait_ge(own_ready, 1)
            pe.wait_ge(loaded, 32)
            for b in range(NS):
                j = b % 2
                if b >= 2:
                    pe.wait_ge(kv_used[j], b // 2)
                for h in range(H):
                    c = slice(h * HG_D, (h + 1) * HG_D)
                    ins = nc.tensor.matmul(ps_kv[j][:, c], k_own[:, b, c], v[:, c], start=True, stop=True)
                ins.then_inc(kv_ready[j], 1)
            for b in range(NS):
                pe.wait_ge(s_ready, b + 1)
                for h in range(H):
                    ins = nc.tensor.matmul(ps_oT[:, h * NS + b:h * NS + b + 1], S[:, b, h, :], q_s[:, h, b:b + 1], start=True, stop=True)
            ins.then_inc(oT_ready, 1)
            pe.wait_ge(oT_copied, 1)
            for h in range(H):
                ins = nc.tensor.transpose(ps_o[0:NS, h * HG_D:(h + 1) * HG_D], oT[:, h, :], ident[:, :])
            ins.then_inc(o_ready, 1)

        @block.vector
        def _(dve):
            dve.wait_ge(consts, 1)
            dve.wait_ge(k_ready, 1)
            nc.vector.tensor_copy(k_nat[:, :], ps_k[0:NS, :])
            dve.drain()
            nc.vector.tensor_tensor(k_own[:, :, :], k_nat[:, :].unsqueeze(1).broadcast_to([NS, NS, HG_WIDTH]),
                                    ident[0:NS, 0:NS].unsqueeze(2).broadcast_to([NS, NS, HG_WIDTH]), ALU.mult).then_inc(own_ready, 1)
            dve.wait_ge(loaded, 32)
            for b in range(NS):
                j = b % 2
                dve.wait_ge(kv_ready[j], b // 2 + 1)
                for h in range(H):
                    nc.vector.scalar_tensor_tensor(out=S[:, b, h, :], in0=S[:, b, h, :], scalar=f_s[:, h, b:b + 1],
                                                   in1=ps_kv[j][:, h * HG_D:(h + 1) * HG_D], op0=ALU.mult, op1=ALU.add)
                dve.drain().then_inc(s_ready, 1)
                dve.sem_inc(kv_used[j], 1)
            dve.wait_ge(oT_ready, 1)
            nc.vector.tensor_copy(oT[:, :, :].rearrange("p h b -> p (h b)"), ps_oT[:, 0:H * NS]).then_inc(oT_copied, 1)
            dve.wait_ge(o_ready, 1)
            nc.vector.tensor_copy(o[:, :], ps_o[0:NS, :]).then_inc(o_copied, 1)


def hgrn(nc, io, scr):
    with ExitStack() as ctx:
        sb = lambda n, s: ctx.enter_context(nc.sbuf_tensor("h_" + n, s, F32))
        factors = sb("factors", [P, N_CHUNK, 4, HG_HEADS, CHUNK])
        decay = sb("decay", [P, N_CHUNK, HG_HEADS])
        f_s, k_s, q_s = (sb(n, [P, HG_HEADS, N_SAMPLE]) for n in ("f_s", "k_s", "q_s"))
        hgrn_gates(nc, io, scr, factors, decay, f_s, k_s, q_s)
        hgrn_steps(nc, io, scr, factors, decay)
        hgrn_sample(nc, io, scr, f_s, k_s, q_s)


def mix_and_route(nc, io, scr):
    o_sb, o_hg, proj, xn_scr, h_scr, score = (scr[n] for n in ("o_sb", "o_hg", "proj", "xn", "h", "score"))
    HALVES = 2 * PEER_HEADS
    Q = 512
    NQ, PER = QW // Q, Q // HALF
    with ExitStack() as ctx:
        sb = lambda n, s, d=F32: ctx.enter_context(nc.sbuf_tensor("mx_" + n, s, d))
        pb = lambda n, s: ctx.enter_context(nc.psum_tensor("mx_" + n, s, F32))
        sem = ctx.enter_context(stage_semaphores(nc, "mx_"))
        w_out, w_pq = sb("w_out", [P, DC, D]), sb("w_pq", [P, DC, QW])
        gain, shift = sb("gain", [P, D]), sb("shift", [P, D])
        mix_gain = sb("mix_gain", [P, D])
        keysT = sb("keysT", [P, HALVES, N_KEYS])
        ident = sb("ident", [P, P])
        in_sb, in_hg, gate, xn = sb("in_sb", [P, 512]), sb("in_hg", [P, 512]), sb("gate", [P, 512]), sb("xn", [P, D])
        squares = sb("squares", [P, 512])
        sums, inv_n, rms = sb("sums", [P, 5]), sb("inv_n", [P, 5]), sb("rms", [P, 5])
        m, mT = sb("m", [P, D]), sb("mT", [P, DC, P])
        pre, h, hT = sb("pre", [P, D]), sb("h", [P, D]), sb("hT", [P, DC, P])
        stats, mv = sb("stats", [P, 12]), sb("mv", [P, 2])
        var, rstd = sb("var", [P, 1]), sb("rstd", [P, 1])
        q, qT, sc = sb("q", [P, 2, Q]), sb("qT", [P, 2, Q]), sb("sc", [P, QW])
        q_stats = sb("q_stats", [P, HALVES, 6])
        q_var, q_rstd, q_tmp = sb("q_var", [P, HALVES]), sb("q_rstd", [P, HALVES]), sb("q_tmp", [P, HALVES])
        minus_half = sb("minus_half", [P, HALVES])
        keys, key_mean = sc, sb("key_mean", [P, HALVES])
        ps_m = pb("ps_m", [P, D])
        ps_t, ps_q, ps_s = ([pb(f"{n}{j}", [P, 512]) for j in range(2)] for n in ("ps_t", "ps_q", "ps_s"))
        weights, consts, keys_ready = sem("weights"), sem("consts"), sem("keys_ready")
        norms, m_whole, keys_centred = sem("norms"), sem("m_whole"), sem("keys_centred")
        in_loaded, in_used = sem("in_loaded"), sem("in_used")
        xn_loaded, xn_used = sem("xn_loaded"), sem("xn_used")
        sq_ready, rms_asked, rms_ready, m_ready, m_used = (sem(n) for n in ("sq_ready", "rms_asked", "rms_ready", "m_ready", "m_used"))
        t_ready, t_used = [sem(f"t_ready{j}") for j in range(2)], [sem(f"t_used{j}") for j in range(2)]
        mT_ready, mix_ready, mix_used = sem("mT_ready"), sem("mix_ready"), sem("mix_used")
        var_ready, rstd_ready, h_ready, h_used, h_done, h_stored = (sem(n) for n in ("var_ready", "rstd_ready", "h_ready", "h_used", "h_done", "h_stored"))
        hT_ready = sem("hT_ready")
        two = lambda n: [sem(f"{n}{j}") for j in range(2)]
        q_ready, q_copied, q_measured, q_used, qT_ready, qT_used, s_ready, s_used = (
            two(n) for n in ("q_ready", "q_copied", "q_measured", "q_used", "qT_ready", "qT_used", "s_ready", "s_used"))
        q_var_ready, q_rstd_ready, sc_ready, sc_stored = sem("q_var_ready"), sem("q_rstd_ready"), sem("sc_ready"), sem("sc_stored")
        block = ctx.enter_context(nc.Block())

        @block.sync
        def _(sp):
            sp.dma_start(keys[:, :].rearrange("k (n c) -> k n c", n=HALVES),
                         io["peer_sub_keys"][0].rearrange("h p k c -> k (h p) c")).then_inc(norms, 16)
            for dst, name in ((gain[:, :], "ln1_g"), (shift[:, :], "ln1_b"),
                              (mix_gain[:, 0:512], "sb_norm_g"), (mix_gain[:, 512:1024], "hg_norm_g")):
                sp.dma_start(dst, io[name][0].partition_broadcast(P)).then_inc(norms, 16)
            sp.dma_start(w_out[:, :, :], io["w_out"][0].rearrange("(c p) n -> p c n", p=P)).then_inc(weights, 16)
            sp.dma_start(w_pq[:, :, :], io["w_pq"][0].rearrange("(c p) n -> p c n", p=P)).then_inc(weights, 16)
            with sp.Fori(0, NB) as b:
                rows = bass.ds(b * P + N_META, P)
                sp.wait_ge(in_used, 1)
                sp.sem_inc(in_used, -1)
                sp.dma_start(in_sb[:, :], o_sb[rows, :]).then_inc(in_loaded, 16)
                sp.dma_start(in_hg[:, :], o_hg[rows, :]).then_inc(in_loaded, 16)
                sp.dma_start(gate[:, :], proj[rows, G_HG:G_HG + HG_WIDTH]).then_inc(in_loaded, 16)
                sp.wait_ge(xn_used, 1)
                sp.sem_inc(xn_used, -1)
                sp.dma_start(xn[:, :], xn_scr[rows, :]).then_inc(xn_loaded, 16)

        @block.gpsimd
        def _(pool):
            identity_matrix(nc, pool, ident[:, :])
            nc.gpsimd.memset(minus_half[:, :], -0.5)
            nc.gpsimd.memset(inv_n[:, 0:1], 1.0 / SB_WIDTH)
            nc.gpsimd.memset(inv_n[:, 1:5], 1.0 / HG_D)
            pool.drain().then_inc(consts, 2)

            def power(out, x, asked, ready):
                pool.wait_ge(asked, 1)
                pool.sem_inc(asked, -1)
                nc.gpsimd.tensor_tensor(out, x, minus_half[:, 0:x.shape[1]], ALU.pow).then_inc(ready, 1)

            mixed = lambda: power(rms[:, :], sums[:, :], rms_asked, rms_ready)
            normed = lambda: power(rstd[:, :], var[:, :], var_ready, rstd_ready)
            queried = lambda: power(q_rstd[:, :], q_var[:, :], q_var_ready, q_rstd_ready)
            mixed(); normed(); mixed()
            with pool.Fori(0, NB - 2) as b:
                normed(); queried(); mixed()
            normed(); queried(); queried()

        @block.scalar
        def _(act):
            act.preload_act_table_set("silu_and_others")

            def measure():
                act.wait_ge(in_loaded, 48)
                act.sem_inc(in_loaded, -48)
                act.wait_ge(m_ready, 1)
                act.sem_inc(m_ready, -1)
                nc.scalar.activation(squares[:, :], in_sb[:, :], ACT.Square, accum_out=sums[:, 0:1])
                act.drain()
                for n in range(HG_HEADS):
                    c = slice(n * HG_D, (n + 1) * HG_D)
                    nc.scalar.activation(squares[:, c], in_hg[:, c], ACT.Square, accum_out=sums[:, n + 1:n + 2])
                nc.scalar.activation(gate[:, :], gate[:, :], ACT.Silu)
                act.drain().then_inc(sq_ready, 1)

            def transposed(dst, ready):
                for j in range(2):
                    act.wait_ge(t_ready[j], 1)
                    act.sem_inc(t_ready[j], -1)
                    nc.scalar.copy(dst[:, 4 * j:4 * j + 4, :], ps_t[j][:, :].rearrange("p (c t) -> p c t", c=4)).then_inc(t_used[j], 1)
                act.drain().then_inc(ready, 1)

            def queries():
                for n in range(NQ + 1):
                    if n < NQ:
                        j = n % 2
                        act.wait_ge(q_ready[j], 1)
                        act.sem_inc(q_ready[j], -1)
                        nc.scalar.copy(q[:, j, :], ps_q[j][:, :])
                        act.drain().then_inc(q_copied[j], 1)
                        act.sem_inc(q_used[j], 1)
                    if n > 0:
                        j = (n - 1) % 2
                        act.wait_ge(t_ready[j], 1)
                        act.sem_inc(t_ready[j], -1)
                        act.wait_ge(qT_used[j], 1)
                        act.sem_inc(qT_used[j], -1)
                        nc.scalar.copy(qT[:, j, :], ps_t[j][:, :])
                        act.drain().then_inc(qT_ready[j], 1)
                        act.sem_inc(t_used[j], 1)

            def store_h(b):
                act.wait_ge(h_done, 1)
                act.sem_inc(h_done, -1)
                act.dma_start(h_scr[bass.ds(b * P, P), :], h[:, :]).then_inc(h_stored, 16)

            def store_scores(b):
                act.wait_ge(sc_ready, 1)
                act.sem_inc(sc_ready, -1)
                act.dma_start(score[bass.ds(b * PEER_HEADS, PEER_HEADS), :, :].rearrange("h t k -> t h k"),
                              sc[:, :].rearrange("t (h k) -> t h k", h=PEER_HEADS)).then_inc(sc_stored, 16)

            act.sem_inc(m_ready, 1)
            for j in range(2):
                act.sem_inc(qT_used[j], 1)
            for half in range(4):
                j = half % 2
                act.wait_ge(t_ready[j], 1)
                act.sem_inc(t_ready[j], -1)
                nc.scalar.copy(keysT[:, 4 * half:4 * half + 4, :].rearrange("p n k -> p (n k)"), ps_t[j][:, :]).then_inc(t_used[j], 1)
            act.drain().then_inc(keys_ready, 1)
            measure()
            transposed(mT, mT_ready)
            measure()
            transposed(hT, hT_ready)
            store_h(0)
            with act.Fori(1, NB - 1) as b:
                transposed(mT, mT_ready)
                measure()
                queries()
                transposed(hT, hT_ready)
                store_h(b)
                store_scores(b - 1)
            transposed(mT, mT_ready)
            queries()
            transposed(hT, hT_ready)
            store_h(NB - 1)
            store_scores(NB - 2)
            queries()
            store_scores(NB - 1)
            act.wait_ge(h_stored, 16)
            act.wait_ge(sc_stored, 16)

        @block.vector
        def _(dve):
            def mix():
                dve.wait_ge(sq_ready, 1)
                dve.sem_inc(sq_ready, -1)
                nc.vector.tensor_tensor(sums[:, :], sums[:, :], inv_n[:, :], ALU.mult)
                dve.drain()
                nc.vector.tensor_scalar(sums[:, :], sums[:, :], EPS, None, ALU.add).then_inc(rms_asked, 1)
                dve.wait_ge(m_used, 1)
                dve.sem_inc(m_used, -1)
                dve.wait_ge(rms_ready, 1)
                dve.sem_inc(rms_ready, -1)
                nc.vector.scalar_tensor_tensor(out=m[:, 0:512], in0=in_sb[:, :], scalar=rms[:, 0:1], in1=mix_gain[:, 0:512],
                                               op0=ALU.mult, op1=ALU.mult)
                for n in range(HG_HEADS):
                    c, d = slice(n * HG_D, (n + 1) * HG_D), slice(512 + n * HG_D, 512 + (n + 1) * HG_D)
                    nc.vector.scalar_tensor_tensor(out=m[:, d], in0=in_hg[:, c], scalar=rms[:, n + 1:n + 2], in1=mix_gain[:, d],
                                                   op0=ALU.mult, op1=ALU.mult)
                dve.drain()
                nc.vector.tensor_tensor(m[:, 512:1024], m[:, 512:1024], gate[:, :], ALU.mult)
                dve.drain().then_inc(m_ready, 1)
                dve.sem_inc(m_whole, 1)
                dve.sem_inc(in_used, 1)

            def residual():
                dve.wait_ge(xn_loaded, 16)
                dve.sem_inc(xn_loaded, -16)
                dve.wait_ge(mix_ready, 1)
                dve.sem_inc(mix_ready, -1)
                nc.vector.scalar_tensor_tensor(out=pre[:, :], in0=xn[:, :], scalar=DN_ALPHA, in1=ps_m[:, :],
                                               op0=ALU.mult, op1=ALU.add)
                dve.drain()
                dve.sem_inc(mix_used, 1)
                dve.sem_inc(xn_used, 1)
                layer_norm_stats(nc, dve, stats, mv[:, :], pre[:, :])
                nc.vector.tensor_scalar(var[:, :], mv[:, 1:2], EPS, None, ALU.add).then_inc(var_ready, 1)
                dve.wait_ge(h_used, 1)
                dve.sem_inc(h_used, -1)
                dve.wait_ge(h_stored, 16)
                dve.sem_inc(h_stored, -16)
                dve.wait_ge(rstd_ready, 1)
                dve.sem_inc(rstd_ready, -1)
                normalise(nc, dve, h[:, :], pre[:, :], mv[:, 0:1], rstd[:, :], gain[:, :], shift[:, :])
                dve.drain().then_inc(h_ready, 1)
                dve.sem_inc(h_done, 1)

            def route():
                for n in range(NQ):
                    j = n % 2
                    dve.wait_ge(q_copied[j], 1)
                    dve.sem_inc(q_copied[j], -1)
                    for k in range(PER):
                        nc.vector.bn_stats(q_stats[:, PER * n + k, :], q[:, j, k * HALF:(k + 1) * HALF])
                    dve.drain().then_inc(q_measured[j], 1)
                nc.vector.tensor_tensor(q_tmp[:, :], q_stats[:, :, 1], q_stats[:, :, 4], ALU.subtract)
                nc.vector.tensor_tensor(q_var[:, :], q_stats[:, :, 2], q_stats[:, :, 5], ALU.add)
                dve.drain()
                nc.vector.tensor_tensor(q_tmp[:, :], q_tmp[:, :], q_tmp[:, :], ALU.mult)
                nc.vector.tensor_scalar(q_var[:, :], q_var[:, :], 1.0 / HALF, EPS, ALU.mult, ALU.add)
                dve.drain()
                nc.vector.scalar_tensor_tensor(out=q_var[:, :], in0=q_tmp[:, :], scalar=0.25, in1=q_var[:, :],
                                               op0=ALU.mult, op1=ALU.add).then_inc(q_var_ready, 1)
                dve.wait_ge(q_rstd_ready, 1)
                dve.sem_inc(q_rstd_ready, -1)
                dve.wait_ge(sc_stored, 16)
                dve.sem_inc(sc_stored, -16)
                for n in range(NQ):
                    j = n % 2
                    dve.wait_ge(s_ready[j], 1)
                    dve.sem_inc(s_ready[j], -1)
                    nc.vector.tensor_tensor(sc[:, n * Q:(n + 1) * Q].rearrange("p (n k) -> p n k", n=PER),
                                            ps_s[j][:, :].rearrange("p (n k) -> p n k", n=PER),
                                            q_rstd[:, PER * n:PER * (n + 1)].unsqueeze(2).broadcast_to([P, PER, N_KEYS]),
                                            ALU.mult).then_inc(s_used[j], 1)
                dve.drain().then_inc(sc_ready, 1)

            for used in (in_used, xn_used, h_used, mix_used, m_used):
                dve.sem_inc(used, 1)
            dve.sem_inc(h_stored, 16)
            dve.wait_ge(norms, 80)
            kv = keys[:, :].rearrange("k (n c) -> k n c", n=HALVES)
            nc.vector.tensor_reduce(key_mean[:, :], kv, AX.X, ALU.add)
            dve.drain()
            nc.vector.tensor_scalar(key_mean[:, :], key_mean[:, :], 1.0 / HALF, None, ALU.mult)
            dve.drain()
            nc.vector.tensor_tensor(kv, kv, key_mean[:, :].unsqueeze(2).broadcast_to([P, HALVES, HALF]), ALU.subtract)
            dve.drain().then_inc(keys_centred, 1)
            dve.wait_ge(keys_ready, 1)
            dve.sem_inc(sc_stored, 16)
            dve.wait_ge(consts, 1)
            mix()
            residual()
            mix()
            with dve.Fori(0, NB - 2) as b:
                residual()
                route()
                mix()
            residual()
            route()
            route()

        @block.tensor
        def _(pe):
            def transposes(src):
                for j in range(2):
                    pe.wait_ge(t_used[j], 1)
                    pe.sem_inc(t_used[j], -1)
                    for c in range(4):
                        ch = 4 * j + c
                        ins = nc.tensor.transpose(ps_t[j][:, c * P:(c + 1) * P], src[:, ch * P:(ch + 1) * P], ident[:, :])
                    ins.then_inc(t_ready[j], 1)

            def project():
                pe.wait_ge(m_whole, 1)
                pe.sem_inc(m_whole, -1)
                transposes(m)
                pe.drain().then_inc(m_used, 1)
                pe.wait_ge(mT_ready, 1)
                pe.sem_inc(mT_ready, -1)
                pe.wait_ge(mix_used, 1)
                pe.sem_inc(mix_used, -1)
                for n in range(2):
                    for c in range(DC):
                        ins = nc.tensor.matmul(ps_m[:, n * 512:(n + 1) * 512], mT[:, c, :], w_out[:, c, n * 512:(n + 1) * 512],
                                               start=(c == 0), stop=(c == DC - 1))
                ins.then_inc(mix_ready, 1)

            def turn_h():
                pe.wait_ge(h_ready, 1)
                pe.sem_inc(h_ready, -1)
                transposes(h)
                pe.drain().then_inc(h_used, 1)

            def route():
                pe.wait_ge(hT_ready, 1)
                pe.sem_inc(hT_ready, -1)
                for n in range(NQ + 2):
                    if n < NQ:
                        j = n % 2
                        pe.wait_ge(q_used[j], 1)
                        pe.sem_inc(q_used[j], -1)
                        for c in range(DC):
                            ins = nc.tensor.matmul(ps_q[j][:, :], hT[:, c, :], w_pq[:, c, n * Q:(n + 1) * Q],
                                                   start=(c == 0), stop=(c == DC - 1))
                        ins.then_inc(q_ready[j], 1)
                    if 1 <= n <= NQ:
                        j = (n - 1) % 2
                        pe.wait_ge(q_measured[j], 1)
                        pe.sem_inc(q_measured[j], -1)
                        pe.wait_ge(t_used[j], 1)
                        pe.sem_inc(t_used[j], -1)
                        for k in range(PER):
                            ins = nc.tensor.transpose(ps_t[j][:, k * P:(k + 1) * P], q[:, j, k * HALF:(k + 1) * HALF], ident[:, :])
                        ins.then_inc(t_ready[j], 1)
                    if n >= 2:
                        j = (n - 2) % 2
                        pe.wait_ge(qT_ready[j], 1)
                        pe.sem_inc(qT_ready[j], -1)
                        pe.wait_ge(s_used[j], 1)
                        pe.sem_inc(s_used[j], -1)
                        for k in range(PER):
                            ins = nc.tensor.matmul(ps_s[j][:, k * N_KEYS:(k + 1) * N_KEYS], qT[:, j, k * P:(k + 1) * P],
                                                   keysT[:, PER * (n - 2) + k, :], start=True, stop=True)
                        ins.then_inc(s_ready[j], 1)
                        pe.drain().then_inc(qT_used[j], 1)

            for j in range(2):
                for used in (t_used, q_used, s_used):
                    pe.sem_inc(used[j], 1)
            pe.wait_ge(consts, 1)
            pe.wait_ge(keys_centred, 1)
            for half in range(4):
                j = half % 2
                pe.wait_ge(t_used[j], 1)
                pe.sem_inc(t_used[j], -1)
                for c in range(4):
                    n = 4 * half + c
                    ins = nc.tensor.transpose(ps_t[j][:, c * P:(c + 1) * P], keys[:, n * HALF:(n + 1) * HALF], ident[:, :])
                ins.then_inc(t_ready[j], 1)
            pe.wait_ge(keys_ready, 1)
            pe.wait_ge(weights, 32)
            project()
            turn_h()
            with pe.Fori(0, NB - 2) as b:
                project()
                route()
                turn_h()
            project()
            route()
            turn_h()
            route()


def experts(nc, io, scr):
    h_scr, score, tail = scr["h"], scr["score"], scr["tail"]
    u_rows, v_rows = io["peer_u"][0], io["peer_v"][0]
    FB = SEQ // P
    PAIRS = PEER_HEADS // 2
    K = TOPK
    with ExitStack() as ctx:
        sb = lambda n, s, d=F32: ctx.enter_context(nc.sbuf_tensor("ex_" + n, s, d))
        pb = lambda n, s: ctx.enter_context(nc.psum_tensor("ex_" + n, s, F32))
        sem = ctx.enter_context(stage_semaphores(nc, "ex_"))
        U, V = [sb(f"U{s}", [P, D]) for s in range(K)], [sb(f"V{s}", [P, D]) for s in range(K)]
        h, h_next, acc, prod = sb("h", [P, D]), sb("h_next", [P, D]), sb("acc", [P, D]), sb("prod", [P, D])
        y = sb("y", [P, D])
        gain, shift = sb("gain", [P, D]), sb("shift", [P, D])
        ident = sb("ident", [P, P])
        sel = sb("sel", [P, N_SAMPLE])
        diag = [sb(f"diag{s}", [P, P]) for s in range(K)]
        iota16 = sb("iota16", [P, K])
        sc = sb("sc", [P, 2, N_KEYS])
        rest = sb("rest", [P, 2 * N_KEYS])
        top, top_i, top_f = sb("top", [P, 2, K]), sb("top_i", [P, 2, K], U32), sb("top_f", [P, 2, K])
        cand, best, best_i = sb("cand", [P, K, K]), sb("best", [P, K]), sb("best_i", [P, K], U32)
        part_i, part_f = sb("part_i", [P, 2, K], U32), sb("part_f", [P, 2, K])
        pick = sb("pick", [P, K, K])
        expert_f = sb("expert_f", [P, 2, K])
        neg_best, e_sum, soft = sb("neg_best", [P, 1]), sb("e_sum", [P, 1]), sb("soft", [P, K])
        expert = [sb(f"expert{u}", [P, K], I32) for u in range(3)]
        gate = [sb(f"gate{u}", [P, K]) for u in range(3)]
        tail_e, tail_g = sb("tail_e", [P, PEER_HEADS, K]), sb("tail_g", [P, PEER_HEADS, K])
        act_in, weight = [sb(f"act_in{u}", [P, K]) for u in range(2)], [sb(f"weight{u}", [P, K]) for u in range(2)]
        stats, mv, var, rstd = sb("stats", [P, 12]), sb("mv", [P, 2]), sb("var", [P, 1]), sb("rstd", [P, 1])
        te_f, te, tg = sb("te_f", [P, PEER_HEADS]), sb("te", [P, PEER_HEADS], I32), sb("tg", [P, PEER_HEADS])
        ps_y = [pb(f"ps_y{u}", [P, D]) for u in range(2)]
        consts, vectors = sem("consts"), sem("vectors")
        sc_loaded, sc_used, h_loaded, h_used = sem("sc_loaded"), sem("sc_used"), sem("h_loaded"), sem("h_used")
        best_ready, exp_ready = sem("best_ready"), sem("exp_ready")
        e_ready = [sem(f"e_ready{u}") for u in range(2)]
        e_used = [sem(f"e_used{u}") for u in range(2)]
        u_loaded, u_used = [sem(f"u_loaded{s}") for s in range(K)], [sem(f"u_used{s}") for s in range(K)]
        v_loaded, v_used = [sem(f"v_loaded{s}") for s in range(K)], [sem(f"v_used{s}") for s in range(K)]
        dots_ready, gelu_ready, weight_ready, weight_used = sem("dots_ready"), sem("gelu_ready"), sem("weight_ready"), sem("weight_used")
        diag_ready, diag_used = [sem(f"diag_ready{s}") for s in range(K)], [sem(f"diag_used{s}") for s in range(K)]
        sums_ready, sums_used = [sem(f"sums_ready{u}") for u in range(2)], [sem(f"sums_used{u}") for u in range(2)]
        var_ready, std_ready, y_ready, y_stored = sem("var_ready"), sem("std_ready"), sem("y_ready"), sem("y_stored")
        tail_ready, tail_stored, tail_loaded, te_ready, th_loaded = (sem(n) for n in ("tail_ready", "tail_stored", "tail_loaded", "te_ready", "th_loaded"))
        tu_loaded, tv_loaded, tdots, tgelu, tdiag, ty = (sem(n) for n in ("tu_loaded", "tv_loaded", "tdots", "tgelu", "tdiag", "ty"))
        main_done = sem("main_done")
        block = ctx.enter_context(nc.Block())

        @block.sync
        def _(sp):
            sp.dma_start(gain[:, :], io["ln2_g"][0].partition_broadcast(P)).then_inc(vectors, 16)
            sp.dma_start(shift[:, :], io["ln2_b"][0].partition_broadcast(P)).then_inc(vectors, 16)

            def load_scores(n):
                sp.wait_ge(sc_used, 1)
                sp.sem_inc(sc_used, -1)
                sp.dma_start(sc[:, :, :].rearrange("t p k -> t (p k)"), score[bass.ds(n, 1), :, :].rearrange("n t k -> t (n k)")).then_inc(sc_loaded, 16)

            def load_block(b):
                sp.wait_ge(h_used, 1)
                sp.sem_inc(h_used, -1)
                sp.dma_start(h_next[:, :], h_scr[bass.ds(b * P, P), :]).then_inc(h_loaded, 16)
                load_scores(b * PEER_HEADS + 1)

            def store_y(b):
                sp.wait_ge(y_ready, 1)
                sp.sem_inc(y_ready, -1)
                sp.dma_start(io["y_prompt"][bass.ds(b * P, P), :], y[:, :]).then_inc(y_stored, 16)

            def load_rest(b):
                load_scores(b * PEER_HEADS + 2)
                load_scores(FB * PEER_HEADS + b)
                with sp.Fori(2, PEER_HEADS) as n:
                    load_scores(b * PEER_HEADS + n + 1)

            load_scores(0)
            load_block(0)
            load_rest(0)
            with sp.Fori(1, FB) as b:
                load_block(b)
                load_scores(b * PEER_HEADS + 2)
                store_y(b - 1)
                load_scores(FB * PEER_HEADS + b)
                with sp.Fori(2, PEER_HEADS) as n:
                    load_scores(b * PEER_HEADS + n + 1)
            store_y(FB - 1)
            sp.wait_ge(tail_ready, 1)
            sp.dma_start(tail[0], tail_e[0:N_SAMPLE, :, :].rearrange("t h k -> t (h k)")).then_inc(tail_stored, 16)
            sp.dma_start(tail[1], tail_g[0:N_SAMPLE, :, :].rearrange("t h k -> t (h k)")).then_inc(tail_stored, 16)
            for t in range(N_SAMPLE):
                sp.dma_start(h[t * K:(t + 1) * K, :], h_scr[FB * P + t, :].partition_broadcast(K)).then_inc(th_loaded, 16)
            sp.dma_start(h_next[0:N_SAMPLE, :], h_scr[FB * P:FB * P + N_SAMPLE, :]).then_inc(th_loaded, 16)
            sp.wait_ge(tail_stored, 32)
            with nc.allow_non_contiguous_dma(reason="1024 words in all"):
                for n, dst in ((0, te_f), (1, tg)):
                    for t in range(N_SAMPLE):
                        sp.dma_start(dst[t * K:(t + 1) * K, :], tail[n, t].rearrange("(h k) -> k h", k=K)).then_inc(tail_loaded, 16)
            sp.wait_ge(y_ready, 1)
            sp.dma_start(io["y_sample"], y[0:N_SAMPLE, :]).then_inc(y_stored, 16)
            sp.wait_ge(y_stored, 16)

        @block.gpsimd
        def _(pool):
            identity_matrix(nc, pool, ident[:, :])
            nc.gpsimd.iota(part_i[:, 0, :].bitcast(I32), pattern=[[1, K]], base=0, channel_multiplier=0)
            nc.gpsimd.memset(sel[:, :], 1.0)
            pool.drain()
            nc.gpsimd.affine_select(out=sel[:, :], in_=sel[:, :], compare_op=ALU.is_ge, fill=0.0, base=0,
                                    pattern=[[-K, N_SAMPLE]], channel_multiplier=1)
            pool.drain()
            nc.gpsimd.affine_select(out=sel[:, :], in_=sel[:, :], compare_op=ALU.is_ge, fill=0.0, base=K - 1,
                                    pattern=[[K, N_SAMPLE]], channel_multiplier=-1)
            pool.drain().then_inc(consts, 2)
            for s in range(K):
                pool.sem_inc(u_used[s], 1)
                pool.sem_inc(v_used[s], 1)

            def gather(dst, rows, idx, used, loaded):
                pool.wait_ge(used, 1)
                pool.sem_inc(used, -1)
                pool.indirect_dma_start(dst[:, :], None, rows, bass.IndirectOffsetOnAxis(ap=idx, axis=0)).then_inc(loaded, 16)

            with pool.Fori(0, FB * PAIRS) as i:
                for u in range(2):
                    pool.wait_ge(e_ready[u], 1)
                    pool.sem_inc(e_ready[u], -1)
                    for s in range(K):
                        gather(U[s], u_rows, expert[u][:, s:s + 1], u_used[s], u_loaded[s])
                    for s in range(K):
                        gather(V[s], v_rows, expert[u][:, s:s + 1], v_used[s], v_loaded[s])
            pool.wait_ge(te_ready, 1)
            for s in range(PEER_HEADS):
                gather(U[s], u_rows, te[:, s:s + 1], u_used[s], tu_loaded)
                gather(V[s], v_rows, te[:, s:s + 1], v_used[s], tv_loaded)

        @block.scalar
        def _(act):
            for s in range(K):
                act.sem_inc(diag_used[s], 1)

            def exps():
                act.wait_ge(best_ready, 1)
                act.sem_inc(best_ready, -1)
                nc.scalar.activation(soft[:, :], best[:, :], ACT.Exp, bias=neg_best[:, :], accum_out=e_sum[:, :])
                act.drain().then_inc(exp_ready, 1)

            def weights(u):
                act.wait_ge(dots_ready, 1)
                act.sem_inc(dots_ready, -1)
                nc.scalar.activation(act_in[u][:, :], act_in[u][:, :], ACT.Gelu).then_inc(gelu_ready, 1)
                act.wait_ge(weight_ready, 1)
                act.sem_inc(weight_ready, -1)
                for s in range(K):
                    act.wait_ge(diag_used[s], 1)
                    act.sem_inc(diag_used[s], -1)
                    nc.scalar.activation(diag[s][:, :], ident[:, :], ACT.Copy, scale=weight[u][:, s:s + 1]).then_inc(diag_ready[s], 1)

            def root():
                act.wait_ge(var_ready, 1)
                act.sem_inc(var_ready, -1)
                nc.scalar.activation(var[:, :], var[:, :], ACT.Sqrt).then_inc(std_ready, 1)

            def steps(first_block):
                weights(0)
                exps()
                if not first_block:
                    root()
                weights(1)
                exps()
                exps()
                with act.Fori(1, PAIRS) as j:
                    for u in range(2):
                        weights(u)
                        exps()

            act.wait_ge(consts, 1)
            exps()
            steps(True)
            with act.Fori(1, FB) as b:
                steps(False)
            root()
            act.wait_ge(tdots, 1)
            nc.scalar.activation(act_in[0][:, 0:PEER_HEADS], act_in[0][:, 0:PEER_HEADS], ACT.Gelu).then_inc(tgelu, 1)
            root()

        @block.tensor
        def _(pe):
            for u in range(2):
                pe.sem_inc(sums_used[u], 1)
            with pe.Fori(0, FB * PAIRS) as i:
                for u in range(2):
                    pe.wait_ge(sums_used[u], 1)
                    pe.sem_inc(sums_used[u], -1)
                    for s in range(K):
                        pe.wait_ge(diag_ready[s], 1)
                        pe.sem_inc(diag_ready[s], -1)
                        pe.wait_ge(v_loaded[s], i * 32 + 16 * (u + 1))
                        for n in range(2):
                            ins = nc.tensor.matmul(ps_y[u][:, n * 512:(n + 1) * 512], diag[s][:, :], V[s][:, n * 512:(n + 1) * 512],
                                                   start=(s == 0), stop=(s == K - 1))
                        ins.then_inc(v_used[s], 1)
                        pe.drain().then_inc(diag_used[s], 1)
                    pe.sem_inc(e_used[u], 1)
                    pe.sem_inc(sums_ready[u], 1)
            pe.wait_ge(sums_used[0], 1)
            pe.wait_ge(tdiag, 1)
            pe.wait_ge(tv_loaded, 16 * PEER_HEADS)
            for s in range(PEER_HEADS):
                for n in range(2):
                    ins = nc.tensor.matmul(ps_y[0][0:N_SAMPLE, n * 512:(n + 1) * 512], diag[s][:, 0:N_SAMPLE], V[s][:, n * 512:(n + 1) * 512],
                                           start=(s == 0), stop=(s == PEER_HEADS - 1))
            ins.then_inc(ty, 1)

        @block.vector
        def _(dve):
            def top16(vals, idx, x, tmp):
                yield lambda: nc.vector.max(vals[:, 0:8], x)
                yield dve.drain
                yield lambda: nc.vector.max_index(idx[:, 0:8], vals[:, 0:8], x)
                yield lambda: nc.vector.match_replace(tmp, vals[:, 0:8], x, LOWEST)
                yield dve.drain
                yield lambda: nc.vector.max(vals[:, 8:16], tmp)
                yield dve.drain
                yield lambda: nc.vector.max_index(idx[:, 8:16], vals[:, 8:16], tmp)

            def route(u):
                bc = [P, K, K]
                def load():
                    dve.wait_ge(sc_loaded, 16)
                    dve.sem_inc(sc_loaded, -16)
                yield load
                for p in range(2):
                    yield from top16(top[:, p, :], top_i[:, p, :], sc[:, p, :], rest[:, 0:N_KEYS])
                    yield dve.drain
                yield lambda: dve.sem_inc(sc_used, 1)
                yield lambda: nc.vector.tensor_tensor(cand[:, :, :], top[:, 0, :].unsqueeze(2).broadcast_to(bc),
                                                      top[:, 1, :].unsqueeze(1).broadcast_to(bc), ALU.add)
                yield lambda: nc.vector.tensor_copy(top_f[:, :, :], top_i[:, :, :])
                yield dve.drain
                flat = cand[:, :, :].rearrange("p a b -> p (a b)")
                yield from top16(best, best_i, flat, rest[:, :])
                yield lambda: nc.vector.tensor_scalar(neg_best[:, :], best[:, 0:1], -1.0, None, ALU.mult)
                yield dve.drain
                yield lambda: dve.sem_inc(best_ready, 1)
                yield lambda: nc.vector.tensor_scalar(part_i[:, 0, :], best_i[:, :], 4, None, ALU.logical_shift_right)
                yield lambda: nc.vector.tensor_scalar(part_i[:, 1, :], best_i[:, :], K - 1, None, ALU.bitwise_and)
                yield dve.drain
                yield lambda: nc.vector.tensor_copy(part_f[:, :, :], part_i[:, :, :])
                yield dve.drain
                for p in range(2):
                    yield lambda p=p: nc.vector.tensor_tensor(pick[:, :, :], part_f[:, p, :].unsqueeze(2).broadcast_to(bc),
                                                              iota16[:, :].unsqueeze(1).broadcast_to(bc), ALU.is_equal)
                    yield dve.drain
                    yield lambda p=p: nc.vector.tensor_tensor(pick[:, :, :], pick[:, :, :], top_f[:, p, :].unsqueeze(1).broadcast_to(bc), ALU.mult)
                    yield dve.drain
                    yield lambda p=p: nc.vector.tensor_reduce(expert_f[:, p, :], pick[:, :, :], AX.X, ALU.add)
                    yield dve.drain
                def choose():
                    if u < 2:
                        dve.wait_ge(e_used[u], 1)
                        dve.sem_inc(e_used[u], -1)
                    nc.vector.scalar_tensor_tensor(out=expert[u][:, :], in0=expert_f[:, 0, :], scalar=float(N_KEYS), in1=expert_f[:, 1, :],
                                                   op0=ALU.mult, op1=ALU.add)
                    dve.drain()
                    if u < 2:
                        dve.sem_inc(e_ready[u], 1)
                yield choose
                def normalise_gates():
                    dve.wait_ge(exp_ready, 1)
                    dve.sem_inc(exp_ready, -1)
                    nc.vector.reciprocal(e_sum[:, :], e_sum[:, :])
                    dve.drain()
                    nc.vector.tensor_scalar(gate[u][:, :], soft[:, :], e_sum[:, :], None, ALU.mult)
                yield normalise_gates

            def layer_norm_2(rows):
                layer_norm_stats(nc, dve, stats[0:rows, :], mv[0:rows, :], acc[0:rows, :])
                nc.vector.tensor_scalar(var[0:rows, :], mv[0:rows, 1:2], EPS, None, ALU.add).then_inc(var_ready, 1)
                dve.wait_ge(std_ready, 1)
                dve.sem_inc(std_ready, -1)
                nc.vector.reciprocal(rstd[0:rows, :], var[0:rows, :])
                dve.wait_ge(y_stored, 16)
                dve.sem_inc(y_stored, -16)
                dve.drain()
                normalise(nc, dve, y[0:rows, :], acc[0:rows, :], mv[0:rows, 0:1], rstd[0:rows, :], gain[0:rows, :], shift[0:rows, :])
                dve.drain().then_inc(y_ready, 1)

            dve.sem_inc(sc_used, 1)
            dve.sem_inc(h_used, 1)
            dve.sem_inc(y_stored, 16)
            for u in range(2):
                dve.sem_inc(e_used[u], 1)
            dve.wait_ge(consts, 1)
            dve.wait_ge(vectors, 32)
            nc.vector.tensor_copy(iota16[:, :], part_i[:, 0, :].bitcast(I32))
            nc.vector.memset(var[:, :], 1.0)
            dve.drain()

            def add_sums(u):
                dve.wait_ge(sums_ready[u], 1)
                dve.sem_inc(sums_ready[u], -1)
                nc.vector.tensor_tensor(acc[:, :], acc[:, :], ps_y[u][:, :], ALU.add)
                dve.drain().then_inc(sums_used[u], 1)

            def step(u, uses, sums_before):
                nxt = list(route(1 - u))
                early = len(nxt) // 4
                for s in range(K):
                    dve.wait_ge(u_loaded[s], uses)
                    nc.vector.tensor_tensor_reduce(out=prod[:, :], in0=U[s][:, :], in1=h[:, :], scale=1.0, scalar=0.0,
                                                   op0=ALU.mult, op1=ALU.add, accum_out=act_in[u][:, s:s + 1]).then_inc(u_used[s], 1)
                    for do in nxt[s * early // K:(s + 1) * early // K]:
                        do()
                    dve.drain()
                dve.sem_inc(dots_ready, 1)
                for do in nxt[early:early + 4]:
                    do()
                dve.wait_ge(gelu_ready, 1)
                dve.sem_inc(gelu_ready, -1)
                nc.vector.tensor_tensor(weight[u][:, :], act_in[u][:, :], gate[u][:, :], ALU.mult)
                dve.drain().then_inc(weight_ready, 1)
                for do in nxt[early + 4:]:
                    do()
                if sums_before:
                    add_sums(1 - u)

            def block_steps(b, first_block):
                dve.wait_ge(h_loaded, 16)
                dve.sem_inc(h_loaded, -16)
                nc.vector.tensor_copy(h[:, :], h_next[:, :])
                dve.drain()
                dve.sem_inc(h_used, 1)
                uses = b * (16 * PEER_HEADS)
                step(0, uses + 16, not first_block)
                if not first_block:
                    layer_norm_2(P)
                nc.vector.tensor_scalar(acc[:, :], h[:, :], DN_ALPHA, None, ALU.mult)
                dve.drain()
                step(1, uses + 32, True)
                for do in route(2):
                    do()
                dve.drain()
                nc.vector.tensor_copy(tail_e[:, bass.ds(b, 1), :].rearrange("p h k -> p (h k)"), expert[2][:, :])
                nc.vector.tensor_copy(tail_g[:, bass.ds(b, 1), :].rearrange("p h k -> p (h k)"), gate[2][:, :])
                dve.drain()
                with dve.Fori(1, PAIRS) as j:
                    for u in range(2):
                        step(u, uses + j * 32 + 16 * (u + 1), True)

            for do in route(0):
                do()
            block_steps(0, True)
            with dve.Fori(1, FB) as b:
                block_steps(b, False)
            add_sums(1)
            layer_norm_2(P)
            dve.sem_inc(tail_ready, 1)
            dve.wait_ge(tail_loaded, 16 * 2 * N_SAMPLE)
            nc.vector.tensor_copy(te[:, :], te_f[:, :])
            dve.drain().then_inc(te_ready, 1)
            dve.wait_ge(th_loaded, 16 * (N_SAMPLE + 1))
            dve.wait_ge(tu_loaded, 16 * PEER_HEADS)
            for s in range(PEER_HEADS):
                nc.vector.tensor_tensor_reduce(out=prod[:, :], in0=U[s][:, :], in1=h[:, :], scale=1.0, scalar=0.0,
                                               op0=ALU.mult, op1=ALU.add, accum_out=act_in[0][:, s:s + 1])
                dve.drain()
            dve.sem_inc(tdots, 1)
            dve.wait_ge(tgelu, 1)
            nc.vector.tensor_tensor(weight[0][:, 0:PEER_HEADS], act_in[0][:, 0:PEER_HEADS], tg[:, :], ALU.mult)
            dve.drain()
            for s in range(PEER_HEADS):
                nc.vector.tensor_scalar(diag[s][:, 0:N_SAMPLE], sel[:, :], weight[0][:, s:s + 1], None, ALU.mult)
            dve.drain().then_inc(tdiag, 1)
            dve.wait_ge(ty, 1)
            nc.vector.scalar_tensor_tensor(out=acc[0:N_SAMPLE, :], in0=h_next[0:N_SAMPLE, :], scalar=DN_ALPHA,
                                           in1=ps_y[0][0:N_SAMPLE, :], op0=ALU.mult, op1=ALU.add)
            dve.drain()
            layer_norm_2(N_SAMPLE)


PHASES = 9


def hybrid_step(nc, io, scr):
    stages = (embed_and_project, sb_prompt, sb_decode, hgrn, mix_and_route, experts)
    for stage in stages[:PHASES]:
        stage(nc, io, scr)


_OUTS = [("y_prompt", (1, SEQ, D)), ("y_sample", (N_SAMPLE, 1, D)),
         ("k_prompt", (1, 1, N_PROMPT, SB_HEADS, SB_DIM)), ("v_prompt", (1, 1, N_PROMPT, SB_HEADS, SB_DIM)),
         ("s_prompt", (1, 1, HG_HEADS, HG_D, HG_D)),
         ("k_sample", (1, N_SAMPLE, 1, SB_HEADS, SB_DIM)), ("v_sample", (1, N_SAMPLE, 1, SB_HEADS, SB_DIM)),
         ("s_sample", (1, N_SAMPLE, HG_HEADS, HG_D, HG_D))]
_VIEWS = {"k_prompt": (N_PROMPT, SB_WIDTH), "v_prompt": (N_PROMPT, SB_WIDTH), "k_sample": (N_SAMPLE, SB_WIDTH),
          "v_sample": (N_SAMPLE, SB_WIDTH), "y_prompt": (SEQ, D), "y_sample": (N_SAMPLE, D),
          "s_prompt": (HG_HEADS, HG_D, HG_D), "s_sample": (N_SAMPLE, HG_HEADS, HG_D, HG_D)}
_SCRATCH = [("xn", (MIX_ROWS, D)), ("proj", (MIX_ROWS, IN_WIDTH)), ("o_sb", (MIX_ROWS, SB_WIDTH)),
            ("o_hg", (MIX_ROWS, HG_WIDTH)), ("h", (NB * P, D)), ("score", (NB * PEER_HEADS + 1, P, 2 * N_KEYS)),
            ("o_heads", (N_SAMPLE * SB_HEADS, SB_WIDTH)), ("tail", (2, N_SAMPLE, PEER_HEADS * TOPK))]
_KIND = "Internal"


def kernel(**inputs):
    import numpy as _np
    import concourse.bacc as _bacc
    from concourse import mybir as _mybir
    from concourse.bass_utils import run_bass_kernel_spmd as _run

    nc = _bacc.Bacc("TRN2", target_bir_lowering=False, num_devices=1)
    arrays, io, scr = {}, {}, {}
    for name, a in inputs.items():
        a = _np.ascontiguousarray(a)
        arrays[f"in_{name}"] = a
        io[name] = nc.dram_tensor(f"in_{name}", a.shape, _mybir.dt.from_np(a.dtype), kind="ExternalInput").ap()
    for name, shape in _OUTS:
        io[name] = nc.dram_tensor(f"out_{name}", _VIEWS[name], _mybir.dt.float32, kind="ExternalOutput").ap()
    for name, shape in _SCRATCH:
        scr[name] = nc.dram_tensor(f"scr_{name}", shape, _mybir.dt.float32, kind=_KIND).ap()
    hybrid_step(nc, io, scr)
    r = _run(nc, [arrays], core_ids=[0])
    return tuple(_np.reshape(r.results[0][f"out_{name}"], shape) for name, shape in _OUTS)
```
